# Optimizing a Trainium2 kernel written in Bass

```python
import jax, jax.numpy as jnp
from jax import lax
import numpy as np

D_MODEL = 2048
BATCH = 1
SEQ = 256
DEPTH = 1
DEC_BATCH = 1
DEC_SEQ = 64
PAST_LEN = 128

CHUNK = 64
WINDOW = 128
WIN_CHUNKS = WINDOW // CHUNK
HEAD_DIM = 64
ATTN_WIDTH = D_MODEL // 2
N_Q_HEADS = ATTN_WIDTH // HEAD_DIM
N_KV_HEADS = N_Q_HEADS // 4
GQA_GROUP = N_Q_HEADS // N_KV_HEADS
KV_WIDTH = N_KV_HEADS * HEAD_DIM
POOL_WINDOWS = (2, 4, 8, 16)
N_POOL_GROUPS = len(POOL_WINDOWS)
POOL_WIDTH = D_MODEL - ATTN_WIDTH
POOL_GROUP_WIDTH = POOL_WIDTH // N_POOL_GROUPS
POOL_HIST = max(POOL_WINDOWS) - 1
D_FF = 4 * D_MODEL
PLE_DIM = 256
IN_WIDTH = ATTN_WIDTH + 2 * KV_WIDTH + POOL_WIDTH + 2 * D_MODEL
NORM_EPS = 1e-6
MASK_VALUE = -1e30

kernel_name = "chunk_causal_swa_sink_pool_hybrid_step"

def rmsnorm(x, g):
    xf = x.astype(jnp.float32)
    xf = xf * lax.rsqrt(jnp.mean(xf * xf, axis=-1, keepdims=True) + NORM_EPS)
    return (xf * g.astype(jnp.float32)).astype(x.dtype)

def alibi_slopes():
    h = np.arange(1, N_Q_HEADS + 1, dtype=np.float32)
    slopes = np.power(np.float32(2.0), -8.0 * h / N_Q_HEADS).astype(np.float32)
    return jnp.asarray(slopes).reshape(N_KV_HEADS, GQA_GROUP)

def block_attn(q, k, v, q_pos, k_pos, sinks):
    s = jnp.einsum('bnqkgd,bnskd->bnkgqs', q, k).astype(jnp.float32) * (HEAD_DIM ** -0.5)
    dist = jnp.abs(q_pos[:, :, None] - k_pos[:, None, :]).astype(jnp.float32)
    s = s - alibi_slopes()[None, None, :, :, None, None] * dist[None, :, None, None]
    qc = q_pos // CHUNK
    kc = k_pos // CHUNK
    valid = ((k_pos[:, None, :] >= 0)
             & (kc[:, None, :] <= qc[:, :, None])
             & (kc[:, None, :] > qc[:, :, None] - WIN_CHUNKS))
    s = jnp.where(valid[None, :, None, None], s, MASK_VALUE)
    sink = jnp.broadcast_to(sinks.astype(jnp.float32).reshape(N_KV_HEADS, GQA_GROUP)[None, None, :, :, None, None],
                            s.shape[:-1] + (1,))
    probs = jax.nn.softmax(jnp.concatenate([s, sink], axis=-1), axis=-1)[..., :-1]
    return jnp.einsum('bnkgqs,bnskd->bnqkgd', probs.astype(v.dtype), v)

def window_attention(q, k, v, hist_k, hist_v, sinks):
    bsz, L = q.shape[0], q.shape[1]
    if hist_k is None:
        nc = L // CHUNK
        qb = q.reshape(bsz, nc, CHUNK, N_KV_HEADS, GQA_GROUP, HEAD_DIM)
        kc = k.reshape(bsz, nc, CHUNK, N_KV_HEADS, HEAD_DIM)
        vc = v.reshape(bsz, nc, CHUNK, N_KV_HEADS, HEAD_DIM)
        pad = jnp.zeros_like(kc[:, :1])
        kb = jnp.concatenate([jnp.concatenate([pad, kc[:, :-1]], axis=1), kc], axis=2)
        vb = jnp.concatenate([jnp.concatenate([pad, vc[:, :-1]], axis=1), vc], axis=2)
        q_pos = jnp.arange(L, dtype=jnp.int32).reshape(nc, CHUNK)
        k_pos = jnp.concatenate([q_pos - CHUNK, q_pos], axis=1)
        new_k, new_v = k[:, -WINDOW:], v[:, -WINDOW:]
    else:
        qb = q.reshape(bsz, 1, L, N_KV_HEADS, GQA_GROUP, HEAD_DIM)
        k_all = jnp.concatenate([hist_k, k], axis=1)
        v_all = jnp.concatenate([hist_v, v], axis=1)
        kb, vb = k_all[:, None], v_all[:, None]
        q_pos = (PAST_LEN + jnp.arange(L, dtype=jnp.int32))[None]
        k_pos = jnp.concatenate([PAST_LEN - WINDOW + jnp.arange(WINDOW, dtype=jnp.int32),
                                 q_pos[0]])[None]
        new_k, new_v = k_all[:, -WINDOW:], v_all[:, -WINDOW:]
    out = block_attn(qb, kb, vb, q_pos, k_pos, sinks)
    return out.reshape(bsz, L, ATTN_WIDTH), new_k, new_v

def pool_mix(u, hist, pos0):
    L = u.shape[1]
    xp = jnp.concatenate([hist, u], axis=1).astype(jnp.float32)
    cs = jnp.concatenate([jnp.zeros_like(xp[:, :1]), jnp.cumsum(xp, axis=1)], axis=1)
    pos = pos0 + jnp.arange(L, dtype=jnp.int32)
    parts = []
    for g, w in enumerate(POOL_WINDOWS):
        sl = slice(g * POOL_GROUP_WIDTH, (g + 1) * POOL_GROUP_WIDTH)
        total = cs[:, POOL_HIST + 1:, sl] - cs[:, POOL_HIST + 1 - w:POOL_HIST + 1 - w + L, sl]
        cnt = jnp.minimum(w, pos + 1).astype(jnp.float32)
        parts.append(total / cnt[None, :, None])
    mean = jnp.concatenate(parts, axis=-1)
    return (mean - u.astype(jnp.float32)).astype(u.dtype)

def trunk_layer(h, p, hist_k, hist_v, hist_u, pos0, lw):
    bsz, L, _ = h.shape
    n1 = rmsnorm(h, lw['g_mix'])
    z = n1 @ lw['w_in']
    o = np.cumsum([0, ATTN_WIDTH, KV_WIDTH, KV_WIDTH, POOL_WIDTH, D_MODEL, D_MODEL])
    q = z[..., o[0]:o[1]].reshape(bsz, L, N_Q_HEADS, HEAD_DIM)
    k = z[..., o[1]:o[2]].reshape(bsz, L, N_KV_HEADS, HEAD_DIM)
    v = z[..., o[2]:o[3]].reshape(bsz, L, N_KV_HEADS, HEAD_DIM)
    u = z[..., o[3]:o[4]]
    g_a = z[..., o[4]:o[5]]
    g_b = z[..., o[5]:o[6]]
    a, new_k, new_v = window_attention(q, k, v, hist_k, hist_v, lw['sinks'])
    a = a @ lw['w_branch_a']
    if hist_u is None:
        hist_u = jnp.zeros((bsz, POOL_HIST, POOL_WIDTH), u.dtype)
        new_u = u[:, -POOL_HIST:]
    else:
        new_u = jnp.concatenate([hist_u, u], axis=1)[:, -POOL_HIST:]
    d = pool_mix(u, hist_u, pos0).reshape(bsz, L, N_POOL_GROUPS, POOL_GROUP_WIDTH)
    d = jnp.einsum('blgc,gce->blge', d, lw['pool_group_w']).reshape(bsz, L, POOL_WIDTH)
    b = (d * lw['pool_scale']) @ lw['w_branch_b']
    m = jax.nn.sigmoid(g_a) * a + jax.nn.sigmoid(g_b) * b
    h = h + m @ lw['w_out']
    hid = rmsnorm(h, lw['g_mlp']) @ lw['w_up']
    h = h + jnp.square(jax.nn.relu(hid)) @ lw['w_down']
    gate = jax.nn.sigmoid(rmsnorm(h, lw['g_ple']) @ lw['w_ple_gate'])
    e = rmsnorm((p @ lw['w_ple_proj']).astype(h.dtype), lw['g_ple_post'])
    h = h + gate * e
    return h, new_k, new_v, new_u

def setup_inputs(seed: int = 0) -> dict:
    key = jax.random.key(seed)
    ks = jax.random.split(key, 24)
    nrm = lambda k, shape, s=1.0: (jax.random.normal(k, shape, jnp.float32) * s)
    gain = lambda k, shape: 1.0 + 0.1 * jax.random.normal(k, shape, jnp.float32)
    return {
        'x_prompt': nrm(ks[0], (BATCH, SEQ, D_MODEL)),
        'x_sample': nrm(ks[1], (DEC_BATCH, DEC_SEQ, D_MODEL)),
        'cache_k': nrm(ks[2], (DEPTH, DEC_BATCH, WINDOW, N_KV_HEADS, HEAD_DIM)),
        'cache_v': nrm(ks[3], (DEPTH, DEC_BATCH, WINDOW, N_KV_HEADS, HEAD_DIM)),
        'state_pool': nrm(ks[4], (DEPTH, DEC_BATCH, POOL_HIST, POOL_WIDTH)),
        'p_prompt': nrm(ks[5], (DEPTH, BATCH, SEQ, PLE_DIM)),
        'p_sample': nrm(ks[6], (DEPTH, DEC_BATCH, DEC_SEQ, PLE_DIM)),
        'g_mix': gain(ks[7], (DEPTH, D_MODEL)),
        'w_in': nrm(ks[8], (DEPTH, D_MODEL, IN_WIDTH), D_MODEL ** -0.5),
        'attn_sinks': nrm(ks[9], (DEPTH, N_Q_HEADS), 0.5),
        'w_branch_a': nrm(ks[10], (DEPTH, ATTN_WIDTH, D_MODEL), ATTN_WIDTH ** -0.5),
        'pool_group_w': nrm(ks[11], (DEPTH, N_POOL_GROUPS, POOL_GROUP_WIDTH, POOL_GROUP_WIDTH), POOL_GROUP_WIDTH ** -0.5),
        'pool_scale': gain(ks[12], (DEPTH, POOL_WIDTH)),
        'w_branch_b': nrm(ks[13], (DEPTH, POOL_WIDTH, D_MODEL), POOL_WIDTH ** -0.5),
        'w_out': nrm(ks[14], (DEPTH, D_MODEL, D_MODEL), D_MODEL ** -0.5),
        'g_mlp': gain(ks[15], (DEPTH, D_MODEL)),
        'w_up': nrm(ks[16], (DEPTH, D_MODEL, D_FF), D_MODEL ** -0.5),
        'w_down': nrm(ks[17], (DEPTH, D_FF, D_MODEL), D_FF ** -0.5),
        'g_ple': gain(ks[18], (DEPTH, D_MODEL)),
        'w_ple_gate': nrm(ks[19], (DEPTH, D_MODEL, D_MODEL), D_MODEL ** -0.5),
        'w_ple_proj': nrm(ks[20], (DEPTH, PLE_DIM, D_MODEL), PLE_DIM ** -0.5),
        'g_ple_post': gain(ks[21], (DEPTH, D_MODEL)),
        'g_final': gain(ks[22], (D_MODEL,)),
    }

def reference(x_prompt, x_sample, cache_k, cache_v, state_pool, p_prompt, p_sample,
              g_mix, w_in, attn_sinks, w_branch_a, pool_group_w, pool_scale, w_branch_b,
              w_out, g_mlp, w_up, w_down, g_ple, w_ple_gate, w_ple_proj, g_ple_post, g_final):
    hp, hs = x_prompt, x_sample
    kp_l, vp_l, up_l, ksl, vsl, usl = [], [], [], [], [], []
    for i in range(DEPTH):
        lw = {'g_mix': g_mix[i], 'w_in': w_in[i], 'sinks': attn_sinks[i],
              'w_branch_a': w_branch_a[i], 'pool_group_w': pool_group_w[i],
              'pool_scale': pool_scale[i], 'w_branch_b': w_branch_b[i], 'w_out': w_out[i],
              'g_mlp': g_mlp[i], 'w_up': w_up[i], 'w_down': w_down[i], 'g_ple': g_ple[i],
              'w_ple_gate': w_ple_gate[i], 'w_ple_proj': w_ple_proj[i], 'g_ple_post': g_ple_post[i]}
        hp, kp, vp, up = trunk_layer(hp, p_prompt[i], None, None, None, 0, lw)
        hs, kk, vv, uu = trunk_layer(hs, p_sample[i], cache_k[i], cache_v[i], state_pool[i], PAST_LEN, lw)
        kp_l.append(kp); vp_l.append(vp); up_l.append(up)
        ksl.append(kk); vsl.append(vv); usl.append(uu)
    y_prompt = rmsnorm(hp, g_final)
    y_sample = rmsnorm(hs, g_final)
    new_k_prompt = jnp.stack(kp_l, 0)
    new_v_prompt = jnp.stack(vp_l, 0)
    new_pool_prompt = jnp.stack(up_l, 0)
    new_k_sample = jnp.stack(ksl, 0)
    new_v_sample = jnp.stack(vsl, 0)
    new_pool_sample = jnp.stack(usl, 0)
    return (y_prompt, y_sample, new_k_prompt, new_v_prompt, new_pool_prompt,
            new_k_sample, new_v_sample, new_pool_sample)


_drawn_inputs = setup_inputs


def setup_inputs(seed=0):
    import zlib

    import numpy as np

    out = dict(_drawn_inputs(seed))
    spreads = {}
    factors = {'attn_sinks': 8.0, 'g_ple': 4.642}
    for name, (base, spread) in spreads.items():
        noise = np.random.default_rng([zlib.crc32(name.encode()), seed]).standard_normal(out[name].shape)
        drawn = base * np.exp(spread * noise) if base else spread * noise
        out[name] = __import__('jax').numpy.asarray(drawn.astype(out[name].dtype))
    for name, factor in factors.items():
        out[name] = (out[name] * factor).astype(out[name].dtype)
    return out
```

```python
from contextlib import ExitStack, contextmanager

import concourse.bass as bass
from concourse import mybir

ALU = mybir.AluOpType
ACT = mybir.ActivationFunctionType
AX = mybir.AxisListType
F32 = mybir.dt.float32
F32R = mybir.dt.float32r

P = 128
D = 2048
SEQ, DEC = 256, 64
T = DEC + SEQ
CHUNK = 64
HD = 64
NH, NKV = 16, 4
FF = 4 * D
PLE = 256
POOL_W = (2, 4, 8, 16)
HIST = max(POOL_W) - 1
EPS = 1e-6
MASK = -1e30

KD = D // P
KA = KD // 2
KP = PLE // P
NPAIR = NKV * HD // P
QPP = KA // NPAIR
FB = 4
KF = FF // P // FB

TILES = 16
UNIT = TILES * P
HALF = UNIT // 2
RAW = 4
SPLIT = 4
BANKS = 4
AHEAD = 2

U_KV = 0
U_Q = U_KV + 2 * NPAIR
U_U = U_Q + KA
U_POOL = U_U + KA
U_MIX = U_POOL + 1
MIX = 6
U_OUT = U_MIX + KA * MIX
U_P0 = U_OUT + KD
U_MLP = U_P0 + 1
U_P1 = U_MLP + FB * 2 * KF
U_GATE = U_P1 + 1
UNITS = U_GATE + KD
C_U = U_U
C_POOL = U_POOL
C_MIX = C_POOL + KA
C_OUT = C_MIX + KA * 8
C_P0 = C_OUT + KD
C_MLP = C_P0 + KD // 2
C_P1 = C_MLP + FB * 2 * KF
C_GATE = C_P1 + KD // 2
assert RAW == 4 and not any(c % BANKS for c in (C_U, C_POOL, C_MIX, C_OUT, C_P0, C_MLP, C_P1, C_GATE))

KX = 3 * CHUNK + SEQ
NB = T // CHUNK
KEYS = 2 * CHUNK


def window(b):
    return 0 if b == 0 else CHUNK * (b + 1)


PL = 2 * HIST + T
PL_S, PL_P = HIST, 2 * HIST + DEC

GROUPS = [(b, p) for b in range(NB) for p in range(NPAIR)]
NG = len(GROUPS)
STEPS = NG + 3
PER_UNIT = (2, 2, 2, 2, 1, 1, 1, 1, 1)
STEPS_AFTER = {U_U + n: range(sum(PER_UNIT[:n]), sum(PER_UNIT[:n + 1])) for n in range(len(PER_UNIT))}
assert sum(PER_UNIT) == STEPS and U_U + len(PER_UNIT) - 1 == U_POOL

DOUBLINGS = [POOL_W[c * P * len(POOL_W) // (KA * P)].bit_length() - 1 for c in range(KA)]
DOUBLED = [sum(DOUBLINGS[:c + 1]) for c in range(KA)]


@contextmanager
def fours(eng, first, end):
    with eng.Fori(0, (end - first) // 4, 1) as k:
        yield k * 4 + first


def small_ready(eng, used, full, u, n, o):
    if o % 4 == 3:
        eng.wait_ge(used, 2 * u + o // 4 + 1)
    else:
        eng.wait_ge(full, 6 * n + 3 * (o // 4) + o % 4 + 1)


def encoder_step(nc, x, cache_k, cache_v, hist, p_in, weights, gains, post_scale, sinks, alibi,
                 inv_count, ident_in, y, kv_prompt, kv_sample, pool_out):
    ctx = ExitStack()
    with ctx:
        def sb(name, cols, dt=F32, on=ctx):
            return on.enter_context(nc.sbuf_tensor(name, [P, cols], dt))

        def psum(name):
            return ctx.enter_context(nc.psum_tensor(name, [P, 512], F32))

        def sem(name):
            return ctx.enter_context(nc.semaphore(name))

        raw = sb("raw", RAW * UNIT)
        w_hi = sb("w_hi", SPLIT * HALF, F32R)
        w_lo = sb("w_lo", SPLIT * HALF, F32R)
        xa_hi, xa_lo = sb("xa_hi", KD * T, F32R), sb("xa_lo", KD * T, F32R)
        h = sb("h", KD * T)
        q = h[:, 0:KA * T]
        kx = h[:, KA * T:KA * T + NPAIR * KX]
        vx = h[:, KA * T + NPAIR * KX:KA * T + 2 * NPAIR * KX]
        with ExitStack() as early:
            d_hi, d_lo = sb("d_hi", KA * T, F32R, early), sb("d_lo", KA * T, F32R, early)
            vt = sb("vt", NB * NPAIR * P, F32, early)
            bias = sb("bias", KA * KEYS, F32, early)
            prob = sb("prob", 3 * QPP * KEYS, F32, early)
            prob_t = sb("prob_t", 2 * QPP * P, F32, early)
            mx, neg, rs, es, rec = (sb(n, NG * QPP, F32, early) for n in ("mx", "neg", "rs", "es", "rec"))
        xb_hi, xb_lo = sb("xb_hi", KD * T, F32R), sb("xb_lo", KD * T, F32R)
        with ExitStack() as early:
            a_hi, a_lo = sb("a_hi", KA * T, F32R, early), sb("a_lo", KA * T, F32R, early)
            b_hi, b_lo = sb("b_hi", KA * T, F32R, early), sb("b_lo", KA * T, F32R, early)
        e = sb("e", KD * T)
        p_raw = sb("p_raw", KP * T)
        p_hi, p_lo = sb("p_hi", KP * T, F32R), sb("p_lo", KP * T, F32R)
        sb("rest_of_branches", 4 * KA * T - KD * T - 3 * KP * T)
        with ExitStack() as early:
            pline = sb("pline", 2 * PL, F32, early)
            pacc = sb("pacc", 2 * PL, F32, early)
            pfix = sb("pfix", HIST, F32, early)
            icnt = sb("icnt", len(POOL_W) * HIST, F32, early)
            hst = sb("hst", KA * HIST, F32, early)
            tail = sb("tail", KA * 2 * HIST, F32, early)
        sg = sb("sg", 4 * T)
        ple = sb("ple", T)
        re = sb("re", T)
        tv = sb("tv", 2 * T)
        sq = sb("sq", 2 * T)
        sumsq, esum = sb("sumsq", T), sb("esum", T)
        r = sb("r", T)
        ones, ident = sb("ones", P), sb("ident", P)
        g_all = sb("g_all", 5 * KD)
        G_MIX, G_MLP, G_PLE, G_POST, G_FIN = range(5)
        pscale = sb("pscale", KA)
        sink = sb("sink", KA)

        def gain(g, c):
            return g_all[:, bass.ds(g * KD + c, 1)]

        def tt(c):
            return bass.ds(c * T, T)

        def duo(t, parity):
            return t[:, parity * T:(parity + 1) * T]

        acc = [psum(f"acc{i}") for i in range(BANKS)]
        s_ps, t_ps, o_ps, m_ps = psum("s_ps"), psum("t_ps"), psum("o_ps"), psum("m_ps")

        raw_in = [sem(f"raw_in{i}") for i in range(RAW)]
        hi_done = sem("hi_done")
        lo_done = sem("lo_done")
        used = sem("used")
        full = sem("full")
        taken = sem("taken")
        x_in = [sem(f"x_in{i}") for i in range(4)]
        gains_in, const_in = sem("gains_in"), sem("const_in")
        kv_cache = sem("kv_cache")
        h_in = sem("h_in")
        p_loaded = sem("p_loaded")
        out_small = sem("out_small")
        y_out = sem("y_out")
        fill = sem("fill")
        xh, xl = sem("xh"), sem("xl")
        xs, xadd = sem("xs"), sem("xadd")
        n_mm = sem("n_mm")
        n_var = sem("n_var")
        n_std = sem("n_std")
        n_r = sem("n_r")
        v_tr, v_copy = sem("v_tr"), sem("v_copy")
        line_a = sem("line_a")
        line_s = sem("line_s")
        dbl = sem("dbl")
        p_d = sem("p_d")
        ph, pl = sem("ph"), sem("pl")
        bh = sem("bh")
        at_qk = sem("at_qk")
        at_s = sem("at_s")
        at_c = sem("at_c")
        at_m = sem("at_m")
        at_e = sem("at_e")
        at_p = sem("at_p")
        at_t, at_tc = sem("at_t"), sem("at_tc")
        at_o = sem("at_o")
        at_h, at_l = sem("at_h"), sem("at_l")
        ms = sem("ms")
        mv = sem("mv")
        mh, ml = sem("mh"), sem("ml")
        fh, fl = sem("fh"), sem("fl")
        fs, fa = sem("fs"), sem("fa")
        hc = sem("hc")
        zero = sem("zero")
        eh, el = sem("eh"), sem("el")
        e_s, e_a = sem("e_s"), sem("e_a")
        uh, ul = sem("uh"), sem("ul")
        gs = sem("gs")
        gv = sem("gv")
        yv = sem("yv")

        CONSTS = 16 * 6
        block = ctx.enter_context(nc.Block())

        @block.sync
        def _(sp):
            def load(u, slot):
                nc.sync.dma_start(raw[:, slot * UNIT:(slot + 1) * UNIT],
                                  weights[bass.ds(u * P, P), :]).then_inc(raw_in[slot], 16)

            for u in range(RAW):
                load(u, u)
            with fours(sp, RAW, UNITS - UNITS % RAW) as u:
                for s in range(RAW):
                    sp.wait_ge(lo_done, 2 * u + (2 * s - 2 * RAW + 2))
                    load(u + s, s)
            for u in range(UNITS - UNITS % RAW, UNITS):
                sp.wait_ge(lo_done, 2 * (u - RAW) + 2)
                load(u, u % RAW)

        @block.gpsimd
        def _(pool):
            n = 0
            for c in range(KA):
                src = pline[:, (c % 2) * PL:(c % 2 + 1) * PL]
                pool.wait_ge(line_a, c + 1)
                pool.wait_ge(taken, C_U + c + 1)
                if c:
                    pool.wait_ge(p_d, 2 * c)
                for k in range(DOUBLINGS[c]):
                    s = 1 << k
                    dst = pacc[:, (k % 2) * PL:(k % 2 + 1) * PL]
                    if k:
                        pool.wait_ge(dbl, n)
                    nc.gpsimd.tensor_tensor(dst[:, 2 * s - 1:PL], src[:, 2 * s - 1:PL], src[:, s - 1:PL - s],
                                            ALU.add).then_inc(dbl, 1)
                    n += 1
                    src = dst

        @block.tensor
        def _(pe):
            def unit(u, parity, chunk, bank, depth, x_hi, x_lo, moving=None, ready=None, inner=False):
                for t in range(TILES):
                    o, k = divmod(t, depth)
                    half = t // 8
                    if t % 8 == 0:
                        pe.wait_ge(lo_done, 2 * u + (half + 1))
                    if k == 0 and not (isinstance(chunk, int) and chunk + o < BANKS):
                        pe.wait_ge(taken, chunk + (o - BANKS + 1))
                    if ready:
                        ready(o, k)
                    at = (2 * parity + half) * HALF + (t % 8) * P
                    out = acc[(bank + o) % BANKS][:, 0:T]
                    m = moving(o, k) if moving else k
                    nc.tensor.matmul(out, w_hi[:, at:at + P], x_hi[:, m * T:(m + 1) * T], start=k == 0, stop=False)
                    nc.tensor.matmul(out, w_hi[:, at:at + P], x_lo[:, m * T:(m + 1) * T], start=False, stop=False)
                    mm = nc.tensor.matmul(out, w_lo[:, at:at + P], x_hi[:, m * T:(m + 1) * T],
                                          start=False, stop=k == depth - 1)
                    if t % 8 == 7:
                        mm.then_inc(used, 1)
                    elif inner and k == depth - 1:
                        mm.then_inc(full, 1)

            def partition_sum(n, src):
                if n:
                    pe.wait_ge(n_var, n)
                nc.tensor.matmul(m_ps[:, 0:T], ones[:, :], src[:, :], start=True, stop=True).then_inc(n_mm, 1)

            def step(i):
                if 0 <= i - 3 < NG:
                    g = i - 3
                    b, p = GROUPS[g]
                    pe.wait_ge(at_tc, g + 1)
                    if g:
                        pe.wait_ge(at_l, g)
                    src = prob_t[:, (g % 2) * QPP * P:(g % 2 + 1) * QPP * P].rearrange(
                        "k (c s t) -> k c s t", c=QPP, s=2)
                    for side in range(2):
                        at = (b * NPAIR + p) * P + side * HD
                        out = o_ps[side * HD:(side + 1) * HD, 0:QPP * CHUNK].rearrange("d (c t) -> d c t", c=QPP)
                        mm = nc.tensor.matmul(out, vt[:, at:at + HD], src[:, :, side, :], start=True, stop=True)
                    mm.then_inc(at_o, 1)
                if 0 <= i - 2 < NG:
                    g = i - 2
                    pe.wait_ge(at_p, g + 1)
                    if g:
                        pe.wait_ge(at_tc, g)
                    for c in range(QPP):
                        at = ((g % 3) * QPP + c) * KEYS
                        mm = nc.tensor.transpose(t_ps[:, c * P:(c + 1) * P], prob[:, at:at + KEYS], ident[:, :])
                    mm.then_inc(at_t, 1)
                if i < NG:
                    b, p = GROUPS[i]
                    if i:
                        pe.wait_ge(at_s, i)
                    else:
                        pe.wait_ge(v_copy, 3)
                        pe.wait_ge(taken, C_U)
                    for c in range(QPP):
                        for side in range(2):
                            rows = slice(side * HD, (side + 1) * HD)
                            qc = (p * QPP + c) * T + b * CHUNK
                            kc = p * KX + window(b)
                            mm = nc.tensor.matmul(s_ps[rows, c * KEYS:(c + 1) * KEYS], q[rows, qc:qc + CHUNK],
                                                  kx[rows, kc:kc + KEYS], start=True, stop=True)
                    mm.then_inc(at_qk, 1)

            for u in range(U_KV, U_Q):
                unit(u, u % 2, u, u % BANKS, KD, xa_hi, xa_lo,
                     ready=(lambda o, k: pe.wait_ge(xl, k + 1)) if u == 0 else None)
                if u == 0:
                    pe.wait_ge(xadd, KD)
                    partition_sum(0, sumsq)
            with fours(pe, U_Q, U_U) as u:
                for s in range(4):
                    unit(u + s, (U_Q + s) % 2, u + s, (U_Q + s) % BANKS, KD, xa_hi, xa_lo)
            pe.wait_ge(taken, U_Q)
            pe.wait_ge(kv_cache, 32)
            pe.wait_ge(const_in, CONSTS)
            for n in range(NB * NPAIR):
                b, p = divmod(n, NPAIR)
                at = p * KX + window(b)
                mm = nc.tensor.transpose((s_ps, t_ps, o_ps)[n // 4][:, (n % 4) * P:(n % 4 + 1) * P],
                                         vx[:, at:at + KEYS], ident[:, :])
                if n % 4 == 3 or n == NB * NPAIR - 1:
                    mm.then_inc(v_tr, 1)
            for u in range(U_U, U_POOL):
                unit(u, u % 2, u, u % BANKS, KD, xa_hi, xa_lo)
                for i in STEPS_AFTER[u]:
                    step(i)
            unit(U_POOL, U_POOL % 2, C_POOL, 0, 2, d_hi, d_lo, moving=lambda o, k: o // 2 * 2 + k,
                 ready=lambda o, k: pe.wait_ge(pl, o // 2 * 2 + k + 1), inner=True)
            for i in STEPS_AFTER[U_POOL]:
                step(i)
            with pe.Fori(0, KA // 2, 1) as j:
                for g in range(2):
                    u, c, par = j * (2 * MIX) + (U_MIX + g * MIX), j * 16 + (C_MIX + g * 8), U_MIX + g * MIX
                    for s in range(4):
                        unit(u + s, (par + s) % 2, c + s, s, KD, xa_hi, xa_lo)
                    pe.wait_ge(at_l, NG)
                    unit(u + 4, (par + 4) % 2, c + 4, 0, KA, a_hi, a_lo)
                    unit(u + 5, (par + 5) % 2, c + 6, 2, KA, b_hi, b_lo)
            with fours(pe, U_OUT, U_P0) as u:
                for s in range(4):
                    unit(u + s, (U_OUT + s) % 2, u + (s + C_OUT - U_OUT), s, KD, xb_hi, xb_lo,
                         ready=(lambda o, k: pe.wait_ge(ml, 2 + k + 1)) if s == 0 else None)

            def embed(u, chunk):
                unit(u, u % 2, chunk, 0, KP, p_hi, p_lo, moving=lambda o, k: k,
                     ready=lambda o, k: pe.wait_ge(el, k + 1), inner=True)

            embed(U_P0, C_P0)
            pe.wait_ge(fa, 2 + KD)
            partition_sum(1, sumsq)
            with pe.Fori(0, FB, 1) as b:
                with fours(pe, 0, KF) as i:
                    for s in range(4):
                        unit(b * (2 * KF) + i + (U_MLP + s), (U_MLP + s) % 2,
                             b * (2 * KF) + i + (C_MLP + s), s, KD, xa_hi, xa_lo,
                             ready=(lambda o, k: pe.wait_ge(fl, k + 1)) if s == 0 else None)
                with fours(pe, 0, KF) as i:
                    for s in range(4):
                        unit(b * (2 * KF) + i + (U_MLP + KF + s), (U_MLP + s) % 2,
                             b * (2 * KF) + i + (C_MLP + KF + s), s, KF, xb_hi, xb_lo,
                             ready=(lambda o, k: pe.wait_ge(ul, b * KF + (2 + k + 1))) if s == 0 else None)
            embed(U_P1, C_P1)
            pe.wait_ge(fa, 2 + 2 * KD)
            partition_sum(2, sumsq)
            pe.wait_ge(e_a, KD)
            partition_sum(3, esum)
            with fours(pe, U_GATE, UNITS) as u:
                for s in range(4):
                    unit(u + s, (U_GATE + s) % 2, u + (s + C_GATE - U_GATE), s, KD, xa_hi, xa_lo,
                         ready=(lambda o, k: pe.wait_ge(fl, KD + k + 1)) if s == 0 else None)
            pe.wait_ge(fa, 2 + 3 * KD)
            partition_sum(4, sumsq)

        @block.scalar
        def _(act):
            def split(u, at):
                slot = at % RAW
                for half in range(2):
                    if half == 0:
                        act.wait_ge(raw_in[slot], rounds(u, at))
                    if not (isinstance(u, int) and u < AHEAD):
                        act.wait_ge(used, 2 * u + (half - SPLIT + 1))
                    dst = (2 * (at % 2) + half) * HALF
                    src = slot * UNIT + half * HALF
                    nc.scalar.activation(w_hi[:, dst:dst + HALF], raw[:, src:src + HALF],
                                         ACT.Copy).then_inc(hi_done, 1)

            def rounds(u, at):
                return 4 * u + (16 - 4 * (at % RAW))

            def ahead(u, at):
                split(u + AHEAD, at + AHEAD)

            def root(n, var):
                act.wait_ge(n_var, n + 1)
                nc.scalar.activation(var[:, :], var[:, :], ACT.Sqrt).then_inc(n_std, 1)

            quarter = 4 * T
            for i in range(4):
                nc.scalar.dma_start(h[:, i * quarter:(i + 1) * quarter],
                                    x[:, i * quarter:(i + 1) * quarter]).then_inc(x_in[i], 16)
                if i == 0:
                    nc.scalar.dma_start(g_all[:, :], gains).then_inc(gains_in, 16)
            for dst, src in ((pscale, post_scale), (sink, sinks), (icnt, inv_count), (ident, ident_in),
                             (hst, hist), (bias, alibi)):
                nc.scalar.dma_start(dst[:, :], src).then_inc(const_in, 16)
            split(0, 0)
            act.wait_ge(gains_in, 16)
            for c in range(KD):
                if c % 4 == 0:
                    act.wait_ge(x_in[c // 4], 16)
                nc.scalar.activation(xa_hi[:, tt(c)], h[:, tt(c)], ACT.Copy, scale=gain(G_MIX, c)).then_inc(xh, 1)
                if c >= 2:
                    act.wait_ge(xadd, c - 1)
                nc.scalar.activation(duo(sq, c % 2), h[:, tt(c)], ACT.Square).then_inc(xs, 1)
            split(1, 1)
            act.wait_ge(xl, KD)
            act.wait_ge(xs, KD)
            for line, cache in ((kx, cache_k), (vx, cache_v)):
                nc.scalar.dma_start(line.rearrange("p (n k) -> p n k", n=NPAIR)[:, :, 0:CHUNK],
                                    cache.rearrange("(n p) k -> p n k", p=P)).then_inc(kv_cache, 16)
            root(0, r)
            for u in range(U_KV, U_Q):
                ahead(u, u)
            with fours(act, U_Q, U_U) as u:
                for s in range(4):
                    ahead(u + s, U_Q + s)
            act.wait_ge(taken, U_Q)
            act.wait_ge(kv_cache, 32)
            for n, line in enumerate((kx, vx)):
                lv = line.rearrange("p (n k) -> p n k", n=NPAIR)
                for dst, cols in ((kv_sample, lv[:, :, 0:KEYS]), (kv_prompt, lv[:, :, KX - KEYS:KX])):
                    nc.scalar.dma_start(dst[n].rearrange("(n p) k -> p n k", p=P), cols).then_inc(out_small, 16)
            for n, bank in enumerate((s_ps, t_ps, o_ps)):
                act.wait_ge(v_tr, n + 1)
                m = min(4, NB * NPAIR - 4 * n) * P
                nc.scalar.activation(vt[:, 4 * n * P:4 * n * P + m], bank[:, 0:m], ACT.Copy).then_inc(v_copy, 1)

            def step(i):
                if 0 <= i - 3 < NG:
                    g = i - 3
                    b, p = GROUPS[g]
                    act.wait_ge(at_o, g + 1)
                    dst = a_hi[:, :].rearrange("p (c t) -> p c t", c=KA)[:, p * QPP:(p + 1) * QPP,
                                                                         b * CHUNK:(b + 1) * CHUNK]
                    nc.scalar.activation(dst, o_ps[:, 0:QPP * CHUNK].rearrange("p (c t) -> p c t", c=QPP),
                                         ACT.Copy).then_inc(at_h, 1)
                if 0 <= i - 2 < NG:
                    g = i - 2
                    act.wait_ge(at_t, g + 1)
                    if g >= 2:
                        act.wait_ge(at_o, g - 1)
                    nc.scalar.activation(prob_t[:, (g % 2) * QPP * P:(g % 2 + 1) * QPP * P], t_ps[:, :],
                                         ACT.Copy).then_inc(at_tc, 1)
                if i < NG:
                    act.wait_ge(at_m, i + 1)
                    for c in range(QPP):
                        at = ((i % 3) * QPP + c) * KEYS
                        n = i * QPP + c
                        nc.scalar.activation(prob[:, at:at + KEYS], prob[:, at:at + KEYS], ACT.Exp,
                                             bias=neg[:, n:n + 1], accum_out=rs[:, n:n + 1])
                    mine = slice(i * QPP, (i + 1) * QPP)
                    nc.scalar.activation(es[:, mine], es[:, mine], ACT.Exp).then_inc(at_e, 1)

            def pool_high(c):
                act.wait_ge(p_d, 2 * c + 2)
                nc.scalar.activation(d_hi[:, tt(c)], duo(tv, c % 2), ACT.Copy).then_inc(ph, 1)

            for u in range(U_U, U_POOL):
                c = u - U_U
                line = pline[:, (c % 2) * PL:(c % 2 + 1) * PL]
                if c == 0:
                    act.wait_ge(const_in, CONSTS)
                if c >= 2:
                    act.wait_ge(p_d, 2 * (c - 1))
                nc.scalar.activation(line[:, 0:HIST], hst[:, c * HIST:(c + 1) * HIST], ACT.Copy).then_inc(line_a, 1)
                act.wait_ge(taken, C_U + c + 1)
                for m, at in enumerate((PL_S + DEC - HIST, PL - HIST)):
                    ins = nc.scalar.activation(tail[:, (2 * c + m) * HIST:(2 * c + m + 1) * HIST],
                                               line[:, at:at + HIST], ACT.Copy)
                ins.then_inc(line_s, 1)
                if c:
                    pool_high(c - 1)
                ahead(u, u)
                for i in STEPS_AFTER[u]:
                    step(i)
            pool_high(KA - 1)
            act.wait_ge(line_s, KA)
            nc.scalar.dma_start(pool_out, tail[:, :]).then_inc(out_small, 16)
            for c in range(KA):
                small_ready(act, used, full, U_POOL, 0, c)
                nc.scalar.activation(b_hi[:, tt(c)], acc[c % BANKS][:, 0:T], ACT.Copy,
                                     scale=pscale[:, c:c + 1]).then_inc(bh, 1)
            ahead(U_POOL, U_POOL)
            for i in STEPS_AFTER[U_POOL]:
                step(i)
            act.wait_ge(at_qk, NG)
            act.wait_ge(out_small, 16 * 5)
            nc.scalar.dma_start(h[:, :], x).then_inc(h_in, 16)

            with act.Fori(0, KA // 2, 1) as jj:
                for g in range(2):
                    at = U_MIX + g * MIX
                    u, j = jj * (2 * MIX) + at, jj * 2 + g
                    for s in range(4):
                        act.wait_ge(taken, j * 8 + (C_MIX + s + 1))
                        nc.scalar.activation(sg[:, tt(s)], sg[:, tt(s)], ACT.Sigmoid).then_inc(ms, 1)
                        ahead(u + s, at + s)
                    ahead(u + 4, at + 4)
                    act.wait_ge(mv, j * 2 + 2)
                    ahead(u + 5, at + 5)
                    for s in range(2):
                        nc.scalar.activation(xb_hi[:, bass.ds((j * 2 + s) * T, T)], sg[:, tt(s)],
                                             ACT.Copy).then_inc(mh, 1)
            act.wait_ge(used, 2 * U_OUT)
            nc.scalar.dma_start(p_raw[:, :], p_in).then_inc(p_loaded, 16)

            def finish(n, c, g, high, parity):
                square(n, parity)
                nc.scalar.activation(high[:, tt(c)], duo(tv, parity), ACT.Copy, scale=gain(g, c)).then_inc(fh, 1)
                nc.scalar.activation(h[:, tt(c)], duo(tv, parity), ACT.Copy).then_inc(hc, 1)

            def square(n, parity):
                act.wait_ge(fa, n + 1)
                nc.scalar.activation(duo(sq, parity), duo(tv, parity), ACT.Square).then_inc(fs, 1)

            with fours(act, 0, KD) as i:
                for s in range(4):
                    act.wait_ge(taken, i + (C_OUT + s + 1))
                    finish(i + s, i + s, G_MLP, xa_hi, s % 2)
                    ahead(i + (U_OUT + s), U_OUT + s)
            act.wait_ge(p_loaded, 16)
            for k in range(KP):
                nc.scalar.activation(p_hi[:, tt(k)], p_raw[:, tt(k)], ACT.Copy).then_inc(eh, 1)

            def embed(u, n):
                for o in range(KD // 2):
                    c = n * (KD // 2) + o
                    small_ready(act, used, full, u, 1 + n, o)
                    if c >= 2:
                        act.wait_ge(e_a, c - 1)
                    nc.scalar.activation(duo(sq, o % 2), acc[o % BANKS][:, 0:T], ACT.Square).then_inc(e_s, 1)
                ahead(u, u)

            act.wait_ge(fa, 2 + KD)
            embed(U_P0, 0)
            root(1, r)
            act.wait_ge(e_a, KD // 2)

            def up(b):
                with fours(act, 0, KF) as i:
                    for s in range(4):
                        u = b * (2 * KF) + i + (U_MLP + s)
                        act.wait_ge(taken, u + (C_MLP - U_MLP + 1))
                        act.wait_ge(ul, b * KF + i + (s + 1))
                        nc.scalar.activation(duo(sq, s % 2), duo(tv, s % 2), ACT.Square)
                        nc.scalar.activation(xb_hi[:, bass.ds((i + s) * T, T)], duo(tv, s % 2),
                                             ACT.Square).then_inc(uh, 1)
                        ahead(u, U_MLP + s)

            with act.Fori(0, FB - 1, 1) as b:
                up(b)
                with fours(act, 0, KF) as i:
                    for s in range(4):
                        ahead(b * (2 * KF) + i + (U_MLP + KF + s), U_MLP + KF + s)
            up(FB - 1)
            act.wait_ge(ul, 2 + FB * KF)
            u_last = U_MLP + (2 * FB - 1) * KF
            with fours(act, 0, KD) as i:
                for s in range(4):
                    act.wait_ge(taken, i + (u_last + C_MLP - U_MLP + s + 1))
                    finish(i + (KD + s), i + s, G_PLE, xa_hi, s % 2)
                    ahead(i + (u_last + s), u_last + s)
            act.wait_ge(fa, 2 + 2 * KD)
            embed(U_P1, 1)
            root(2, r)
            root(3, re)
            act.wait_ge(e_a, KD)

            def gate(n, parity):
                act.wait_ge(taken, n + (C_GATE + 1))
                nc.scalar.activation(duo(tv, parity), duo(tv, parity), ACT.Sigmoid).then_inc(gs, 1)
                act.wait_ge(gv, 3 * n + 3)
                square(n + 2 * KD, parity)
                nc.scalar.activation(h[:, tt(n)], duo(tv, parity), ACT.Copy, scale=gain(G_FIN, n)).then_inc(hc, 1)

            with fours(act, 0, KD - 4) as i:
                for s in range(4):
                    gate(i + s, s % 2)
                    ahead(i + (U_GATE + s), U_GATE + s)
            for c in range(KD - 4, KD):
                gate(c, c % 2)
                if c < KD - AHEAD:
                    ahead(U_GATE + c, U_GATE + c)
            root(4, r)
            for i in range(4):
                act.wait_ge(yv, i + 1)
                nc.scalar.dma_start(y[:, i * quarter:(i + 1) * quarter],
                                    h[:, i * quarter:(i + 1) * quarter]).then_inc(y_out, 16)
            act.wait_ge(y_out, 64)

        @block.vector
        def _(dve):
            def split(u, at):
                for half in range(2):
                    dve.wait_ge(hi_done, 2 * u + (half + 1))
                    dst = (2 * (at % 2) + half) * HALF
                    src = (at % RAW) * UNIT + half * HALF
                    nc.vector.tensor_tensor(w_lo[:, dst:dst + HALF], raw[:, src:src + HALF],
                                            w_hi[:, dst:dst + HALF], ALU.subtract).then_inc(lo_done, 1)

            def ahead(u, at):
                split(u + AHEAD, at + AHEAD)

            def factor(n, out):
                dve.wait_ge(n_mm, n + 1)
                nc.vector.tensor_scalar(out[:, :], m_ps[:, 0:T], 1.0 / D, EPS, ALU.mult, ALU.add).then_inc(n_var, 1)
                dve.wait_ge(n_std, n + 1)
                nc.vector.reciprocal(out[:, :], out[:, :]).then_inc(n_r, 1)
                dve.wait_ge(n_r, n + 1)

            def clear_sum(n):
                nc.vector.memset(sumsq[:, :], 0.0).then_inc(zero, 1)
                dve.wait_ge(zero, n + 1)

            nc.vector.memset(ones[:, :], 1.0).then_inc(hc, 2)
            dve.wait_ge(hc, 2)
            nc.vector.memset(sumsq[:, :], 0.0).then_inc(fill, 1)
            nc.vector.memset(esum[:, :], 0.0).then_inc(ml, 2)
            dve.wait_ge(ml, 2)
            nc.vector.memset(pline[:, PL_P - HIST:PL_P], 0.0).then_inc(fa, 2)
            nc.vector.memset(pline[:, PL + PL_P - HIST:PL + PL_P], 0.0).then_inc(ul, 2)
            dve.wait_ge(fill, 1)
            dve.wait_ge(fa, 2)
            dve.wait_ge(ul, 2)
            split(0, 0)
            for c in range(KD):
                dve.wait_ge(xh, c + 1)
                nc.vector.scalar_tensor_tensor(out=xa_lo[:, tt(c)], in0=h[:, tt(c)], scalar=gain(G_MIX, c),
                                               in1=xa_hi[:, tt(c)], op0=ALU.mult, op1=ALU.subtract).then_inc(xl, 1)
                dve.wait_ge(xs, c + 1)
                if c:
                    dve.wait_ge(xadd, c)
                nc.vector.tensor_tensor(sumsq[:, :], sumsq[:, :], duo(sq, c % 2), ALU.add).then_inc(xadd, 1)
            split(1, 1)
            factor(0, r)
            clear_sum(0)
            for n, line in enumerate((kx, vx)):
                for p in range(NPAIR):
                    u = n * NPAIR + p
                    dve.wait_ge(used, 2 * u + 2)
                    at = p * KX
                    nc.vector.memset(line[:, at + 2 * CHUNK:at + 3 * CHUNK], 0.0)
                    nc.vector.tensor_tensor(line[:, at + CHUNK:at + 2 * CHUNK], acc[u][:, 0:DEC], r[:, 0:DEC], ALU.mult)
                    nc.vector.tensor_tensor(line[:, at + 3 * CHUNK:at + KX], acc[u][:, DEC:T], r[:, DEC:T],
                                            ALU.mult).then_inc(taken, 1)
                    ahead(u, u)
            with fours(dve, U_Q, U_U) as u:
                for s in range(4):
                    dve.wait_ge(used, 2 * u + (2 * s + 2))
                    nc.vector.tensor_tensor(q[:, bass.ds((u + (s - U_Q)) * T, T)], acc[(U_Q + s) % BANKS][:, 0:T],
                                            r[:, :], ALU.mult).then_inc(taken, 1)
                    ahead(u + s, U_Q + s)

            small = [0]

            def link(ins):
                small[0] += 1
                ins.then_inc(at_c, 1)
                dve.wait_ge(at_c, small[0])

            def step(i):
                if 0 <= i - 3 < NG:
                    g = i - 3
                    b, p = GROUPS[g]
                    dve.wait_ge(at_h, g + 1)
                    rows, cols = slice(p * QPP, (p + 1) * QPP), slice(b * CHUNK, (b + 1) * CHUNK)
                    nc.vector.tensor_tensor(a_lo[:, :].rearrange("p (c t) -> p c t", c=KA)[:, rows, cols],
                                            o_ps[:, 0:QPP * CHUNK].rearrange("p (c t) -> p c t", c=QPP),
                                            a_hi[:, :].rearrange("p (c t) -> p c t", c=KA)[:, rows, cols],
                                            ALU.subtract).then_inc(at_l, 1)
                if 0 <= i - 1 < NG:
                    g = i - 1
                    mine = slice(g * QPP, (g + 1) * QPP)
                    dve.wait_ge(at_e, g + 1)
                    link(nc.vector.tensor_tensor(rs[:, mine], rs[:, mine], es[:, mine], ALU.add))
                    link(nc.vector.reciprocal(rec[:, mine], rs[:, mine]))
                    pg = prob[:, (g % 3) * QPP * KEYS:(g % 3 + 1) * QPP * KEYS].rearrange("p (c k) -> p c k", c=QPP)
                    nc.vector.tensor_tensor(pg, pg, rec[:, mine].unsqueeze(2).broadcast_to([P, QPP, KEYS]),
                                            ALU.mult).then_inc(at_p, 1)
                if i < NG:
                    b, p = GROUPS[i]
                    mine = slice(i * QPP, (i + 1) * QPP)
                    pg = prob[:, (i % 3) * QPP * KEYS:(i % 3 + 1) * QPP * KEYS]
                    pg3 = pg.rearrange("p (c k) -> p c k", c=QPP)
                    dve.wait_ge(at_qk, i + 1)
                    if i >= 3:
                        dve.wait_ge(at_t, i - 2)
                    nc.vector.scalar_tensor_tensor(
                        out=pg, in0=s_ps[:, :], scalar=HD ** -0.5,
                        in1=bias[:, p * QPP * KEYS:(p + 1) * QPP * KEYS], op0=ALU.mult, op1=ALU.add).then_inc(at_s, 1)
                    dve.wait_ge(at_s, i + 1)
                    if b == 1:
                        link(nc.vector.memset(pg3[:, :, 0:CHUNK], MASK))
                    link(nc.vector.tensor_reduce(mx[:, mine], pg3, AX.X, ALU.max))
                    link(nc.vector.tensor_tensor(mx[:, mine], mx[:, mine], sink[:, p * QPP:(p + 1) * QPP], ALU.max))
                    link(nc.vector.tensor_scalar(neg[:, mine], mx[:, mine], -1.0, None, ALU.mult))
                    nc.vector.tensor_tensor(es[:, mine], sink[:, p * QPP:(p + 1) * QPP], neg[:, mine],
                                            ALU.add).then_inc(at_m, 1)

            def pool_mean(c):
                w = POOL_W[c // 2]
                line = pline[:, (c % 2) * PL:(c % 2 + 1) * PL]
                k = (DOUBLINGS[c] - 1) % 2
                sums = pacc[:, k * PL:(k + 1) * PL]
                out = duo(tv, c % 2)
                dve.wait_ge(dbl, DOUBLED[c])
                for a, z in ((PL_S, PL_S + DEC), (PL_P + HIST, PL)):
                    nc.vector.scalar_tensor_tensor(
                        out=out[:, a - HIST:z - HIST] if a == PL_S else out[:, DEC + HIST:T], in0=sums[:, a:z],
                        scalar=1.0 / w, in1=line[:, a:z], op0=ALU.mult, op1=ALU.subtract)
                g = c // 2
                nc.vector.tensor_tensor(pfix[:, :], sums[:, PL_P:PL_P + HIST], icnt[:, g * HIST:(g + 1) * HIST],
                                        ALU.mult).then_inc(p_d, 1)
                dve.wait_ge(p_d, 2 * c + 1)
                nc.vector.tensor_tensor(out[:, DEC:DEC + HIST], pfix[:, :], line[:, PL_P:PL_P + HIST],
                                        ALU.subtract).then_inc(p_d, 1)

            def pool_low(c):
                dve.wait_ge(ph, c + 1)
                nc.vector.tensor_tensor(d_lo[:, tt(c)], duo(tv, c % 2), d_hi[:, tt(c)], ALU.subtract).then_inc(pl, 1)

            dve.wait_ge(const_in, CONSTS)
            for u in range(U_U, U_POOL):
                c = u - U_U
                dve.wait_ge(used, 2 * u + 2)
                if c >= 2:
                    dve.wait_ge(line_s, c - 1)
                line = pline[:, (c % 2) * PL:(c % 2 + 1) * PL]
                ps = acc[u % BANKS]
                nc.vector.tensor_tensor(line[:, PL_S:PL_S + DEC], ps[:, 0:DEC], r[:, 0:DEC], ALU.mult)
                nc.vector.tensor_tensor(line[:, PL_P:PL], ps[:, DEC:T], r[:, DEC:T], ALU.mult).then_inc(taken, 1)
                if c:
                    pool_mean(c - 1)
                    pool_low(c - 1)
                ahead(u, u)
                for i in STEPS_AFTER[u]:
                    step(i)
            pool_mean(KA - 1)
            pool_low(KA - 1)
            for c in range(KA):
                dve.wait_ge(bh, c + 1)
                nc.vector.scalar_tensor_tensor(out=b_lo[:, tt(c)], in0=acc[c % BANKS][:, 0:T], scalar=pscale[:, c:c + 1],
                                               in1=b_hi[:, tt(c)], op0=ALU.mult, op1=ALU.subtract).then_inc(taken, 1)
            ahead(U_POOL, U_POOL)
            for i in STEPS_AFTER[U_POOL]:
                step(i)

            with dve.Fori(0, KA // 2, 1) as jj:
                for g in range(2):
                    at = U_MIX + g * MIX
                    u, j = jj * (2 * MIX) + at, jj * 2 + g
                    c0 = j * 8 + C_MIX
                    dve.wait_ge(ml, j * 2 + 2)
                    for s in range(4):
                        dve.wait_ge(used, 2 * u + (2 * s + 2))
                        nc.vector.tensor_tensor(sg[:, tt(s)], acc[s][:, 0:T], r[:, :], ALU.mult).then_inc(taken, 1)
                        ahead(u + s, at + s)
                    for s in range(2):
                        dve.wait_ge(used, 2 * u + (2 * 4 + s + 1))
                        dve.wait_ge(ms, j * 4 + (s + 1))
                        nc.vector.tensor_tensor(sg[:, tt(s)], acc[s][:, 0:T], sg[:, tt(s)], ALU.mult).then_inc(taken, 1)
                    ahead(u + 4, at + 4)
                    for s in range(2):
                        dve.wait_ge(used, 2 * u + (2 * 5 + s + 1))
                        dve.wait_ge(ms, j * 4 + (2 + s + 1))
                        nc.vector.tensor_tensor(sg[:, tt(2 + s)], acc[2 + s][:, 0:T], sg[:, tt(2 + s)],
                                                ALU.mult).then_inc(taken, 1)
                        dve.wait_ge(taken, c0 + (6 + s + 1))
                        nc.vector.tensor_tensor(sg[:, tt(s)], sg[:, tt(s)], sg[:, tt(2 + s)], ALU.add).then_inc(mv, 1)
                    ahead(u + 5, at + 5)
                    for s in range(2):
                        dve.wait_ge(mh, j * 2 + (s + 1))
                        m = bass.ds((j * 2 + s) * T, T)
                        nc.vector.tensor_tensor(xb_lo[:, m], sg[:, tt(s)], xb_hi[:, m], ALU.subtract).then_inc(ml, 1)

            def residual(c, bank, out):
                nc.vector.tensor_tensor(out, h[:, tt(c)], acc[bank][:, 0:T], ALU.add).then_inc(taken, 1)

            def finish(n, c, g, high, low, parity):
                dve.wait_ge(fh, n + 1)
                nc.vector.scalar_tensor_tensor(out=low[:, tt(c)], in0=duo(tv, parity), scalar=gain(g, c),
                                               in1=high[:, tt(c)], op0=ALU.mult, op1=ALU.subtract).then_inc(fl, 1)
                add_square(n, parity)

            def add_square(n, parity):
                dve.wait_ge(fs, n + 1)
                dve.wait_ge(fa, n + 2)
                nc.vector.tensor_tensor(sumsq[:, :], sumsq[:, :], duo(sq, parity), ALU.add).then_inc(fa, 1)

            dve.wait_ge(h_in, 16)
            with fours(dve, 0, KD) as i:
                for s in range(4):
                    c = i + s
                    dve.wait_ge(used, 2 * i + (2 * (U_OUT + s) + 2))
                    dve.wait_ge(hc, c + 1)
                    residual(c, s, duo(tv, s % 2))
                    finish(c, c, G_MLP, xa_hi, xa_lo, s % 2)
                    ahead(i + (U_OUT + s), U_OUT + s)
            for k in range(KP):
                dve.wait_ge(eh, k + 1)
                nc.vector.tensor_tensor(p_lo[:, tt(k)], p_raw[:, tt(k)], p_hi[:, tt(k)], ALU.subtract).then_inc(el, 1)

            def embed(u, n):
                for o in range(KD // 2):
                    c = n * (KD // 2) + o
                    dve.wait_ge(e_s, c + 1)
                    if c:
                        dve.wait_ge(e_a, c)
                    nc.vector.tensor_tensor(esum[:, :], esum[:, :], duo(sq, o % 2), ALU.add).then_inc(e_a, 1)
                    nc.vector.tensor_copy(e[:, tt(c)], acc[o % BANKS][:, 0:T]).then_inc(taken, 1)
                ahead(u, u)

            embed(U_P0, 0)
            factor(1, r)
            clear_sum(1)

            def up(b):
                with fours(dve, 0, KF) as i:
                    for s in range(4):
                        u = b * (2 * KF) + i + (U_MLP + s)
                        dve.wait_ge(used, 2 * u + 2)
                        nc.vector.scalar_tensor_tensor(out=duo(tv, s % 2), in0=acc[s][:, 0:T], scalar=0.0,
                                                       in1=r[:, :], op0=ALU.max, op1=ALU.mult).then_inc(taken, 1)
                        dve.wait_ge(uh, b * KF + i + (s + 1))
                        m = bass.ds((i + s) * T, T)
                        nc.vector.tensor_tensor(xb_lo[:, m], duo(sq, s % 2), xb_hi[:, m], ALU.subtract).then_inc(ul, 1)
                        ahead(u, U_MLP + s)

            with dve.Fori(0, FB - 1, 1) as b:
                up(b)
                with fours(dve, 0, KF) as i:
                    for s in range(4):
                        u = b * (2 * KF) + i + (U_MLP + KF + s)
                        dve.wait_ge(used, 2 * u + 2)
                        residual(i + s, s, h[:, tt(i + s)])
                        ahead(u, U_MLP + KF + s)
            up(FB - 1)
            u_last = U_MLP + (2 * FB - 1) * KF
            with fours(dve, 0, KD) as i:
                for s in range(4):
                    dve.wait_ge(used, 2 * i + (2 * (u_last + s) + 2))
                    dve.wait_ge(hc, i + (KD + s + 1))
                    residual(i + s, s, duo(tv, s % 2))
                    finish(i + (KD + s), i + s, G_PLE, xa_hi, xa_lo, s % 2)
                    ahead(i + (u_last + s), u_last + s)
            embed(U_P1, 1)
            factor(2, r)
            clear_sum(2)
            factor(3, re)

            def ple_chunk(n, bank):
                parity = bank % 2
                dve.wait_ge(hc, n + (2 * KD + 1))
                dve.wait_ge(used, 2 * n + (2 * U_GATE + 2))
                nc.vector.tensor_tensor(duo(tv, parity), acc[bank][:, 0:T], r[:, :], ALU.mult).then_inc(taken, 1)
                nc.vector.scalar_tensor_tensor(out=ple[:, :], in0=e[:, tt(n)], scalar=gain(G_POST, n), in1=re[:, :],
                                               op0=ALU.mult, op1=ALU.mult).then_inc(gv, 1)
                dve.wait_ge(gv, 3 * n + 1)
                dve.wait_ge(gs, n + 1)
                nc.vector.tensor_tensor(ple[:, :], ple[:, :], duo(tv, parity), ALU.mult).then_inc(gv, 1)
                dve.wait_ge(gv, 3 * n + 2)
                nc.vector.tensor_tensor(duo(tv, parity), h[:, tt(n)], ple[:, :], ALU.add).then_inc(gv, 1)
                add_square(n + 2 * KD, parity)

            with fours(dve, 0, KD - 4) as i:
                for s in range(4):
                    ple_chunk(i + s, s)
                    ahead(i + (U_GATE + s), U_GATE + s)
            for c in range(KD - 4, KD):
                ple_chunk(c, c % BANKS)
                if c < KD - AHEAD:
                    ahead(U_GATE + c, U_GATE + c)
            factor(4, r)
            dve.wait_ge(hc, 2 + 3 * KD)
            for i in range(4):
                part = h[:, i * 4 * T:(i + 1) * 4 * T].rearrange("p (c t) -> p c t", c=4)
                nc.vector.tensor_tensor(part, part, r[:, :].unsqueeze(1).broadcast_to([P, 4, T]),
                                        ALU.mult).then_inc(yv, 1)


def _tiles(w, np):
    i, o = w.shape
    return w.reshape(i // P, P, o // P, P).transpose(2, 1, 0, 3)


def _units(w, np):
    t = _tiles(w, np)
    per = TILES // t.shape[2]
    n = t.shape[0] // per
    return t.reshape(n, per, P, t.shape[2], P).transpose(0, 2, 1, 3, 4).reshape(n, P, UNIT)


def kernel(**inputs):
    import numpy as np
    import concourse.bacc as bacc
    from concourse.bass_utils import run_bass_kernel_spmd

    a = {k: np.asarray(v) for k, v in inputs.items()}

    heads = [8 * p + 4 * s + c for p in range(NPAIR) for c in range(QPP) for s in range(2)]
    qcols = np.concatenate([np.arange(hd * HD, (hd + 1) * HD) for hd in heads])
    w_in = a["w_in"][0]
    o = np.cumsum([0, NH * HD, NKV * HD, NKV * HD, KA * P, D, D])
    part = [w_in[:, o[n]:o[n + 1]] for n in range(6)]
    ga, gb = _units(part[4], np), _units(part[5], np)
    ba, bb = _units(a["w_branch_a"][0][qcols], np), _units(a["w_branch_b"][0], np)
    stream = [_units(part[1], np), _units(part[2], np), _units(part[0][:, qcols], np), _units(part[3], np)]
    pg = a["pool_group_w"][0].reshape(len(POOL_W), 2, P, 2, P).transpose(2, 0, 3, 1, 4)
    stream.append(pg.reshape(1, P, UNIT))
    for j in range(KA):
        stream += [ga[2 * j:2 * j + 2], gb[2 * j:2 * j + 2], ba[j:j + 1], bb[j:j + 1]]
    stream.append(_units(a["w_out"][0], np))
    proj = _units(a["w_ple_proj"][0], np)
    stream.append(proj[0:1])
    up = _units(a["w_up"][0], np)
    down = a["w_down"][0].reshape(FB, FF // FB, D)
    for b in range(FB):
        stream += [up[b * KF:(b + 1) * KF], _units(down[b], np)]
    stream += [proj[1:2], _units(a["w_ple_gate"][0], np)]
    weights = np.concatenate(stream).reshape(UNITS * P, UNIT)

    def feature_major(s, p):
        t = np.concatenate([s, p]).T
        return np.ascontiguousarray(t.reshape(-1, P, T).transpose(1, 0, 2)).reshape(P, -1)

    def cols(v):
        return v.reshape(-1, P).T

    slope = np.power(np.float32(2.0), np.float32(-8.0) * np.arange(1, NH + 1, dtype=np.float32) / NH)
    dist = np.abs(CHUNK + np.arange(CHUNK)[:, None] - np.arange(KEYS)[None, :]).astype(np.float32)
    alibi = np.stack([-slope[hd] * dist for hd in heads]).astype(np.float32)
    alibi = alibi.reshape(KA, 2 * CHUNK, KEYS).transpose(1, 0, 2).reshape(P, KA * KEYS)
    count = np.minimum(np.array(POOL_W)[:, None], np.arange(1, HIST + 1)[None, :])
    inv_count = np.broadcast_to((1.0 / count).astype(np.float32).reshape(1, -1), (P, len(POOL_W) * HIST))
    sinks = a["attn_sinks"][0][heads].reshape(KA, 2)
    sinks = np.repeat(sinks[:, :, None], CHUNK, axis=2).reshape(KA, P).T

    def cached(c):
        return c[0, 0].reshape(KEYS, NKV * HD)[CHUNK:].T

    arrays = {
        "x": feature_major(a["x_sample"][0], a["x_prompt"][0]),
        "cache_k": cached(a["cache_k"]), "cache_v": cached(a["cache_v"]),
        "hist": a["state_pool"][0, 0].T.reshape(KA, P, HIST).transpose(1, 0, 2).reshape(P, -1),
        "p_in": feature_major(a["p_sample"][0, 0], a["p_prompt"][0, 0]),
        "weights": weights,
        "gains": np.concatenate([cols(a["g_mix"][0]), cols(a["g_mlp"][0]), cols(a["g_ple"][0]),
                                 cols(a["g_ple_post"][0]), cols(a["g_final"])], axis=1),
        "post_scale": cols(a["pool_scale"][0]), "sinks": sinks, "alibi": alibi, "inv_count": inv_count,
        "ident_in": np.eye(P, dtype=np.float32),
    }
    outs = {"y": (P, KD * T), "kv_prompt": (2, NPAIR * P, KEYS), "kv_sample": (2, NPAIR * P, KEYS),
            "pool_out": (P, KA * 2 * HIST)}

    nc = bacc.Bacc("TRN2", target_bir_lowering=False, num_devices=1, dynamic_dma_scratch_size=1024)
    args, sent = {}, {}
    for name, v in arrays.items():
        v = np.ascontiguousarray(v)
        sent[f"in_{name}"] = v
        args[name] = nc.dram_tensor(f"in_{name}", v.shape, mybir.dt.from_np(v.dtype), kind="ExternalInput").ap()
    for name, shape in outs.items():
        args[name] = nc.dram_tensor(f"out_{name}", shape, F32, kind="ExternalOutput").ap()
    encoder_step(nc, **args)
    got = run_bass_kernel_spmd(nc, [sent], core_ids=[0]).results[0]

    yt = got["out_y"].reshape(P, KD, T).transpose(2, 1, 0).reshape(T, D)

    def rows(v):
        return v.T.reshape(1, 1, KEYS, NKV, HD)

    pool = got["out_pool_out"].reshape(P, KA, 2, HIST).transpose(2, 3, 1, 0).reshape(2, 1, 1, HIST, KA * P)
    kp, ks = got["out_kv_prompt"], got["out_kv_sample"]
    res = (yt[DEC:].reshape(1, SEQ, D), yt[:DEC].reshape(1, DEC, D), rows(kp[0]), rows(kp[1]), pool[1],
           rows(ks[0]), rows(ks[1]), pool[0])
    return tuple(np.ascontiguousarray(v) for v in res)
```

```python
from contextlib import ExitStack, contextmanager

import concourse.bass as bass
from concourse import mybir

ALU = mybir.AluOpType
ACT = mybir.ActivationFunctionType
AX = mybir.AxisListType
F32 = mybir.dt.float32
F32R = mybir.dt.float32r

P = 128
D = 2048
SEQ, DEC = 256, 64
T = DEC + SEQ
CHUNK = 64
HD = 64
NH, NKV = 16, 4
FF = 4 * D
PLE = 256
POOL_W = (16, 8, 4, 2)
HIST = max(POOL_W) - 1
EPS = 1e-6
MASK = -1e30

KD = D // P
KA = KD // 2
KP = PLE // P
NPAIR = NKV * HD // P
QPP = KA // NPAIR
FB = 4
KF = FF // P // FB

TILES = 16
UNIT = TILES * P
HALF = UNIT // 2
RAW = 4
SPLIT = 4
BANKS = 4
AHEAD = 2

U_KV = 0
U_Q = U_KV + 2 * NPAIR
U_U = U_Q + KA
U_POOL = U_U + KA
U_MIX = U_POOL + 1
MIX = 6
U_OUT = U_MIX + KA * MIX
U_P0 = U_OUT + KD
U_MLP = U_P0 + 1
U_P1 = U_MLP + (FB - 1) * 2 * KF
U_LAST = U_P1 + 1
U_GATE = U_LAST + 2 * KF
UNITS = U_GATE + KD
C_U = U_U
C_POOL = U_POOL
C_MIX = C_POOL + KA
C_OUT = C_MIX + KA * 8
C_P0 = C_OUT + KD
C_MLP = C_P0 + KD // 2
C_P1 = C_MLP + (FB - 1) * 2 * KF
C_LAST = C_P1 + KD // 2
C_GATE = C_LAST + 2 * KF
assert RAW == 4 and not any(c % BANKS for c in (C_U, C_POOL, C_MIX, C_OUT, C_P0, C_MLP, C_P1, C_LAST, C_GATE))

KX = 3 * CHUNK + SEQ
NB = T // CHUNK
KEYS = 2 * CHUNK


def window(b):
    return 0 if b == 0 else CHUNK * (b + 1)


PL = 2 * HIST + T
PL_S, PL_P = HIST, 2 * HIST + DEC

GROUPS = [(b, p) for p in range(NPAIR) for b in range(NB)]
NG = len(GROUPS)
STEPS = NG + 3
U_STEP = U_Q + QPP
assert U_STEP + STEPS - 1 == U_POOL

DOUBLINGS = [POOL_W[c * P * len(POOL_W) // (KA * P)].bit_length() - 1 for c in range(KA)]
DOUBLED = [sum(DOUBLINGS[:c + 1]) for c in range(KA)]


@contextmanager
def fours(eng, first, end):
    with eng.Fori(0, (end - first) // 4, 1) as k:
        yield k * 4 + first


Y_PARTS = ((0, 2), (2, 6), (6, 11), (11, KD))


def small_ready(eng, used, full, u, n, o):
    if o % 4 == 3:
        eng.wait_ge(used, 2 * u + o // 4 + 1)
    else:
        eng.wait_ge(full, 6 * n + 3 * (o // 4) + o % 4 + 1)


def encoder_step(nc, x, cache_k, cache_v, hist, p_in, weights, gains, post_scale, sinks, alibi,
                 inv_count, ident_in, y, kv_prompt, kv_sample, pool_out):
    ctx = ExitStack()
    with ctx:
        def sb(name, cols, dt=F32, on=ctx):
            return on.enter_context(nc.sbuf_tensor(name, [P, cols], dt))

        def psum(name):
            return ctx.enter_context(nc.psum_tensor(name, [P, 512], F32))

        def sem(name):
            return ctx.enter_context(nc.semaphore(name))

        raw = sb("raw", RAW * UNIT)
        w_hi = sb("w_hi", SPLIT * HALF, F32R)
        w_lo = sb("w_lo", SPLIT * HALF, F32R)
        xa_hi, xa_lo = sb("xa_hi", KD * T, F32R), sb("xa_lo", KD * T, F32R)
        h = sb("h", KD * T)
        q = h[:, 0:KA * T]
        kx = h[:, KA * T:KA * T + NPAIR * KX]
        vx = h[:, KA * T + NPAIR * KX:KA * T + 2 * NPAIR * KX]
        with ExitStack() as early:
            d_hi, d_lo = sb("d_hi", KA * T, F32R, early), sb("d_lo", KA * T, F32R, early)
            vt = sb("vt", NB * NPAIR * P, F32, early)
            bias = sb("bias", KA * KEYS, F32, early)
            prob = sb("prob", 3 * QPP * KEYS, F32, early)
            prob_t = sb("prob_t", 2 * QPP * P, F32, early)
            mx, neg, rs, es, rec = (sb(n, NG * QPP, F32, early) for n in ("mx", "neg", "rs", "es", "rec"))
        xb_hi, xb_lo = sb("xb_hi", KD * T, F32R), sb("xb_lo", KD * T, F32R)
        with ExitStack() as early:
            a_hi, a_lo = sb("a_hi", KA * T, F32R, early), sb("a_lo", KA * T, F32R, early)
            b_hi, b_lo = sb("b_hi", KA * T, F32R, early), sb("b_lo", KA * T, F32R, early)
        e = sb("e", KD * T)
        p_raw = sb("p_raw", KP * T)
        p_hi, p_lo = sb("p_hi", KP * T, F32R), sb("p_lo", KP * T, F32R)
        sb("rest_of_branches", 4 * KA * T - KD * T - 3 * KP * T)
        with ExitStack() as early:
            pline = sb("pline", 2 * PL, F32, early)
            pacc = sb("pacc", 2 * PL, F32, early)
            pfix = sb("pfix", HIST, F32, early)
            icnt = sb("icnt", len(POOL_W) * HIST, F32, early)
            hst = sb("hst", KA * HIST, F32, early)
            tail = sb("tail", KA * 2 * HIST, F32, early)
        sg = sb("sg", 4 * T)
        ple = sb("ple", T)
        re = sb("re", T)
        tv = sb("tv", 2 * T)
        sq = sb("sq", 2 * T)
        sumsq, esum = sb("sumsq", T), sb("esum", T)
        r = sb("r", T)
        ones, ident = sb("ones", P), sb("ident", P)
        g_all = sb("g_all", 5 * KD)
        G_MIX, G_MLP, G_PLE, G_POST, G_FIN = range(5)
        pscale = sb("pscale", KA)
        sink = sb("sink", KA)

        def gain(g, c):
            return g_all[:, bass.ds(g * KD + c, 1)]

        def tt(c):
            return bass.ds(c * T, T)

        def duo(t, parity):
            return t[:, parity * T:(parity + 1) * T]

        acc = [psum(f"acc{i}") for i in range(BANKS)]
        s_ps, t_ps, o_ps, m_ps = psum("s_ps"), psum("t_ps"), psum("o_ps"), psum("m_ps")

        raw_in = [sem(f"raw_in{i}") for i in range(RAW)]
        hi_done = sem("hi_done")
        lo_done = sem("lo_done")
        used = sem("used")
        full = sem("full")
        taken = sem("taken")
        x_in = [sem(f"x_in{i}") for i in range(4)]
        gains_in, const_in = sem("gains_in"), sem("const_in")
        kv_cache = sem("kv_cache")
        h_in = sem("h_in")
        p_loaded = sem("p_loaded")
        out_small = sem("out_small")
        y_out = sem("y_out")
        fill = sem("fill")
        xh, xl = sem("xh"), sem("xl")
        xs, xadd = sem("xs"), sem("xadd")
        n_mm = sem("n_mm")
        n_var = sem("n_var")
        n_std = sem("n_std")
        n_r = sem("n_r")
        v_tr, v_copy = sem("v_tr"), sem("v_copy")
        line_a = sem("line_a")
        line_s = sem("line_s")
        dbl = sem("dbl")
        p_d = sem("p_d")
        ph, pl = sem("ph"), sem("pl")
        bh = sem("bh")
        at_qk = sem("at_qk")
        at_s = sem("at_s")
        at_c = sem("at_c")
        at_m = sem("at_m")
        at_e = sem("at_e")
        at_p = sem("at_p")
        at_t, at_tc = sem("at_t"), sem("at_tc")
        at_o = sem("at_o")
        at_h, at_l = sem("at_h"), sem("at_l")
        ms = sem("ms")
        mv = sem("mv")
        ml = sem("ml")
        fh, fl = sem("fh"), sem("fl")
        fs, fa = sem("fs"), sem("fa")
        hc = sem("hc")
        zero = sem("zero")
        eh, el = sem("eh"), sem("el")
        e_s = sem("e_s")
        uh, ul = sem("uh"), sem("ul")
        gs = sem("gs")
        gv = sem("gv")
        yv = sem("yv")

        CONSTS = 16 * 6
        block = ctx.enter_context(nc.Block())

        @block.sync
        def _(sp):
            def load(u, slot):
                nc.sync.dma_start(raw[:, slot * UNIT:(slot + 1) * UNIT],
                                  weights[bass.ds(u * P, P), :]).then_inc(raw_in[slot], 16)

            def load_x(i):
                part = slice(i * 4 * T, (i + 1) * 4 * T)
                nc.sync.dma_start(h[:, part], x[:, part]).then_inc(x_in[i], 16)

            load_x(0)
            load(0, 0)
            for i in range(1, 4):
                load_x(i)
            for u in range(1, RAW):
                load(u, u)
            with fours(sp, RAW, UNITS - UNITS % RAW) as u:
                for s in range(RAW):
                    sp.wait_ge(lo_done, 2 * u + (2 * s - 2 * RAW + 2))
                    load(u + s, s)
            for u in range(UNITS - UNITS % RAW, UNITS):
                sp.wait_ge(lo_done, 2 * (u - RAW) + 2)
                load(u, u % RAW)

        @block.gpsimd
        def _(pool):
            n = 0
            for c in range(KA):
                src = pline[:, (c % 2) * PL:(c % 2 + 1) * PL]
                pool.wait_ge(line_a, c + 1)
                pool.wait_ge(taken, C_U + c + 1)
                if c:
                    pool.wait_ge(p_d, 2 * c)
                for k in range(DOUBLINGS[c]):
                    s = 1 << k
                    dst = pacc[:, (k % 2) * PL:(k % 2 + 1) * PL]
                    if k:
                        pool.wait_ge(dbl, n)
                    nc.gpsimd.tensor_tensor(dst[:, 2 * s - 1:PL], src[:, 2 * s - 1:PL], src[:, s - 1:PL - s],
                                            ALU.add).then_inc(dbl, 1)
                    n += 1
                    src = dst

        @block.tensor
        def _(pe):
            def unit(u, parity, chunk, bank, depth, x_hi, x_lo, moving=None, ready=None, inner=False):
                for t in range(TILES):
                    o, k = divmod(t, depth)
                    half = t // 8
                    if t % 8 == 0:
                        pe.wait_ge(lo_done, 2 * u + (half + 1))
                    if k == 0 and not (isinstance(chunk, int) and chunk + o < BANKS):
                        pe.wait_ge(taken, chunk + (o - BANKS + 1))
                    if ready:
                        ready(o, k)
                    at = (2 * parity + half) * HALF + (t % 8) * P
                    out = acc[(bank + o) % BANKS][:, 0:T]
                    m = moving(o, k) if moving else k
                    nc.tensor.matmul(out, w_hi[:, at:at + P], x_hi[:, m * T:(m + 1) * T], start=k == 0, stop=False)
                    nc.tensor.matmul(out, w_hi[:, at:at + P], x_lo[:, m * T:(m + 1) * T], start=False, stop=False)
                    mm = nc.tensor.matmul(out, w_lo[:, at:at + P], x_hi[:, m * T:(m + 1) * T],
                                          start=False, stop=k == depth - 1)
                    if t % 8 == 7:
                        mm.then_inc(used, 1)
                    elif inner and k == depth - 1:
                        mm.then_inc(full, 1)

            def partition_sum(n, src):
                if n:
                    pe.wait_ge(n_var, n)
                nc.tensor.matmul(m_ps[:, 0:T], ones[:, :], src[:, :], start=True, stop=True).then_inc(n_mm, 1)

            def step(i):
                if 0 <= i - 3 < NG:
                    g = i - 3
                    b, p = GROUPS[g]
                    pe.wait_ge(at_tc, g + 1)
                    if g:
                        pe.wait_ge(at_l, g)
                    src = prob_t[:, (g % 2) * QPP * P:(g % 2 + 1) * QPP * P].rearrange(
                        "k (c s t) -> k c s t", c=QPP, s=2)
                    for side in range(2):
                        at = (b * NPAIR + p) * P + side * HD
                        out = o_ps[side * HD:(side + 1) * HD, 0:QPP * CHUNK].rearrange("d (c t) -> d c t", c=QPP)
                        mm = nc.tensor.matmul(out, vt[:, at:at + HD], src[:, :, side, :], start=True, stop=True)
                    mm.then_inc(at_o, 1)
                if 0 <= i - 2 < NG:
                    g = i - 2
                    pe.wait_ge(at_p, g + 1)
                    if g:
                        pe.wait_ge(at_tc, g)
                    for c in range(QPP):
                        at = ((g % 3) * QPP + c) * KEYS
                        mm = nc.tensor.transpose(t_ps[:, c * P:(c + 1) * P], prob[:, at:at + KEYS], ident[:, :])
                    mm.then_inc(at_t, 1)
                if i < NG:
                    b, p = GROUPS[i]
                    if i:
                        pe.wait_ge(at_s, i)
                    else:
                        pe.wait_ge(v_copy, 3)
                    if b == 0:
                        pe.wait_ge(taken, U_Q + (p + 1) * QPP)
                    for c in range(QPP):
                        for side in range(2):
                            rows = slice(side * HD, (side + 1) * HD)
                            qc = (p * QPP + c) * T + b * CHUNK
                            kc = p * KX + window(b)
                            mm = nc.tensor.matmul(s_ps[rows, c * KEYS:(c + 1) * KEYS], q[rows, qc:qc + CHUNK],
                                                  kx[rows, kc:kc + KEYS], start=True, stop=True)
                    mm.then_inc(at_qk, 1)

            for u in range(U_KV, U_STEP):
                unit(u, u % 2, u, u % BANKS, KD, xa_hi, xa_lo,
                     ready=(lambda o, k: pe.wait_ge(xl, k + 1)) if u == 0 else None)
                if u == 2:
                    pe.wait_ge(xadd, KD)
                    partition_sum(0, sumsq)
            pe.wait_ge(taken, U_Q)
            pe.wait_ge(kv_cache, 32)
            pe.wait_ge(const_in, CONSTS)
            for n in range(NB * NPAIR):
                b, p = divmod(n, NPAIR)
                at = p * KX + window(b)
                mm = nc.tensor.transpose((s_ps, t_ps, o_ps)[n // 4][:, (n % 4) * P:(n % 4 + 1) * P],
                                         vx[:, at:at + KEYS], ident[:, :])
                if n % 4 == 3 or n == NB * NPAIR - 1:
                    mm.then_inc(v_tr, 1)
            for u in range(U_STEP, U_POOL):
                unit(u, u % 2, u, u % BANKS, KD, xa_hi, xa_lo)
                step(u - U_STEP)
            unit(U_POOL, U_POOL % 2, C_POOL, 0, 2, d_hi, d_lo, moving=lambda o, k: o // 2 * 2 + k,
                 ready=lambda o, k: pe.wait_ge(pl, o // 2 * 2 + k + 1), inner=True)
            step(STEPS - 1)
            with pe.Fori(0, KA // 2, 1) as j:
                for g in range(2):
                    u, c, par = j * (2 * MIX) + (U_MIX + g * MIX), j * 16 + (C_MIX + g * 8), U_MIX + g * MIX
                    for s in range(4):
                        unit(u + s, (par + s) % 2, c + s, s, KD, xa_hi, xa_lo)
                    pe.wait_ge(at_l, NG)
                    unit(u + 4, (par + 4) % 2, c + 4, 0, KA, a_hi, a_lo)
                    unit(u + 5, (par + 5) % 2, c + 6, 2, KA, b_hi, b_lo)
            with fours(pe, U_OUT, U_P0) as u:
                for s in range(4):
                    unit(u + s, (U_OUT + s) % 2, u + (s + C_OUT - U_OUT), s, KD, xb_hi, xb_lo,
                         ready=(lambda o, k: pe.wait_ge(ml, 2 + k + 1)) if s == 0 else None)

            def embed(u, chunk):
                unit(u, u % 2, chunk, 0, KP, p_hi, p_lo, moving=lambda o, k: k,
                     ready=lambda o, k: pe.wait_ge(el, k + 1), inner=True)

            embed(U_P0, C_P0)
            pe.wait_ge(fa, 2 + KD)
            partition_sum(1, sumsq)
            def up_down(u0, c0, n):
                with fours(pe, 0, KF) as i:
                    for s in range(4):
                        unit(i + u0 + s, par(s), i + c0 + s, s, KD, xa_hi, xa_lo,
                             ready=(lambda o, k: pe.wait_ge(fl, k + 1)) if s == 0 else None)
                with fours(pe, 0, KF) as i:
                    for s in range(4):
                        unit(i + u0 + (KF + s), par(s), i + c0 + (KF + s), s, KF, xb_hi, xb_lo,
                             ready=(lambda o, k: pe.wait_ge(ul, n + (2 + k + 1))) if s == 0 else None)

            par = lambda s: (U_MLP + s) % 2
            with pe.Fori(0, FB - 1, 1) as b:
                up_down(b * (2 * KF) + U_MLP, b * (2 * KF) + C_MLP, b * KF)
            embed(U_P1, C_P1)
            par = lambda s: (U_LAST + s) % 2
            up_down(U_LAST, C_LAST, (FB - 1) * KF)
            def gate(u, s, ready=None):
                unit(u + s, (U_GATE + s) % 2, u + (s + C_GATE - U_GATE), s, KD, xa_hi, xa_lo, ready=ready)

            for s in range(4):
                gate(U_GATE, s, (lambda o, k: pe.wait_ge(fl, KD + k + 1)) if s == 0 else None)
                if s == 0:
                    pe.wait_ge(fa, 2 + 2 * KD)
                    partition_sum(2, sumsq)
                    partition_sum(3, esum)
            with fours(pe, U_GATE + 4, UNITS) as u:
                for s in range(4):
                    gate(u, s)
            pe.wait_ge(fa, 2 + 3 * KD)
            partition_sum(4, sumsq)

        @block.scalar
        def _(act):
            def split(u, at, halves=range(2)):
                slot = at % RAW
                for half in halves:
                    if half == 0:
                        act.wait_ge(raw_in[slot], rounds(u, at))
                    if not (isinstance(u, int) and u < AHEAD):
                        act.wait_ge(used, 2 * u + (half - SPLIT + 1))
                    dst = (2 * (at % 2) + half) * HALF
                    src = slot * UNIT + half * HALF
                    nc.scalar.activation(w_hi[:, dst:dst + HALF], raw[:, src:src + HALF],
                                         ACT.Copy).then_inc(hi_done, 1)

            def rounds(u, at):
                return 4 * u + (16 - 4 * (at % RAW))

            def ahead(u, at, halves=range(2)):
                split(u + AHEAD, at + AHEAD, halves)

            def root(n, var, out):
                act.wait_ge(n_var, n + 1)
                nc.scalar.activation(out[:, :], var[:, :], ACT.Sqrt).then_inc(n_std, 1)

            nc.scalar.dma_start(g_all[:, :], gains).then_inc(gains_in, 16)
            for dst, src in ((pscale, post_scale), (sink, sinks), (icnt, inv_count), (ident, ident_in),
                             (hst, hist), (bias, alibi)):
                nc.scalar.dma_start(dst[:, :], src).then_inc(const_in, 16)
            act.wait_ge(gains_in, 16)
            for c in range(KD):
                if c % 4 == 0:
                    act.wait_ge(x_in[c // 4], 16)
                nc.scalar.activation(xa_hi[:, tt(c)], h[:, tt(c)], ACT.Copy, scale=gain(G_MIX, c)).then_inc(xh, 1)
                if c in (3, 7):
                    split(0, 0, [c // 4])
            split(1, 1)
            for c in range(KD):
                if c >= 2:
                    act.wait_ge(xadd, c - 1)
                nc.scalar.activation(duo(sq, c % 2), h[:, tt(c)], ACT.Square).then_inc(xs, 1)
                if c == KD // 2:
                    ahead(0, 0)
            act.wait_ge(xl, KD)
            act.wait_ge(xs, KD)
            for line, cache in ((kx, cache_k), (vx, cache_v)):
                nc.scalar.dma_start(line.rearrange("p (n k) -> p n k", n=NPAIR)[:, :, 0:CHUNK],
                                    cache.rearrange("(n p) k -> p n k", p=P)).then_inc(kv_cache, 16)
            ahead(1, 1)
            root(0, sumsq, r)
            for u in range(2, U_STEP):
                ahead(u, u)
            act.wait_ge(taken, U_Q)
            act.wait_ge(kv_cache, 32)
            for n, line in enumerate((kx, vx)):
                lv = line.rearrange("p (n k) -> p n k", n=NPAIR)
                for dst, cols in ((kv_sample, lv[:, :, 0:KEYS]), (kv_prompt, lv[:, :, KX - KEYS:KX])):
                    nc.scalar.dma_start(dst[n].rearrange("(n p) k -> p n k", p=P), cols).then_inc(out_small, 16)
            for n, bank in enumerate((s_ps, t_ps, o_ps)):
                act.wait_ge(v_tr, n + 1)
                m = min(4, NB * NPAIR - 4 * n) * P
                nc.scalar.activation(vt[:, 4 * n * P:4 * n * P + m], bank[:, 0:m], ACT.Copy).then_inc(v_copy, 1)

            def step(i):
                if 0 <= i - 3 < NG:
                    g = i - 3
                    b, p = GROUPS[g]
                    act.wait_ge(at_o, g + 1)
                    dst = a_hi[:, :].rearrange("p (c t) -> p c t", c=KA)[:, p * QPP:(p + 1) * QPP,
                                                                         b * CHUNK:(b + 1) * CHUNK]
                    nc.scalar.activation(dst, o_ps[:, 0:QPP * CHUNK].rearrange("p (c t) -> p c t", c=QPP),
                                         ACT.Copy).then_inc(at_h, 1)
                if 0 <= i - 2 < NG:
                    g = i - 2
                    act.wait_ge(at_t, g + 1)
                    if g >= 2:
                        act.wait_ge(at_o, g - 1)
                    nc.scalar.activation(prob_t[:, (g % 2) * QPP * P:(g % 2 + 1) * QPP * P], t_ps[:, :],
                                         ACT.Copy).then_inc(at_tc, 1)
                if i < NG:
                    act.wait_ge(at_m, i + 1)
                    for c in range(QPP):
                        at = ((i % 3) * QPP + c) * KEYS
                        n = i * QPP + c
                        nc.scalar.activation(prob[:, at:at + KEYS], prob[:, at:at + KEYS], ACT.Exp,
                                             bias=neg[:, n:n + 1], accum_out=rs[:, n:n + 1])
                    mine = slice(i * QPP, (i + 1) * QPP)
                    nc.scalar.activation(es[:, mine], es[:, mine], ACT.Exp).then_inc(at_e, 1)

            def pool_high(c):
                act.wait_ge(p_d, 2 * c + 2)
                nc.scalar.activation(d_hi[:, tt(c)], duo(tv, c % 2), ACT.Copy).then_inc(ph, 1)

            for u in range(U_STEP, U_U):
                ahead(u, u)
                step(u - U_STEP)
            act.wait_ge(const_in, CONSTS)
            for u in range(U_U, U_POOL):
                c = u - U_U
                line = pline[:, (c % 2) * PL:(c % 2 + 1) * PL]
                if c >= 2:
                    act.wait_ge(p_d, 2 * (c - 1))
                nc.scalar.activation(line[:, 0:HIST], hst[:, c * HIST:(c + 1) * HIST], ACT.Copy).then_inc(line_a, 1)
                act.wait_ge(taken, C_U + c + 1)
                for m, at in enumerate((PL_S + DEC - HIST, PL - HIST)):
                    ins = nc.scalar.activation(tail[:, (2 * c + m) * HIST:(2 * c + m + 1) * HIST],
                                               line[:, at:at + HIST], ACT.Copy)
                ins.then_inc(line_s, 1)
                if c:
                    pool_high(c - 1)
                if c < KA - 1:
                    ahead(u, u)
                    step(u - U_STEP)
            pool_high(KA - 1)
            step(STEPS - 2)
            act.wait_ge(line_s, KA)
            nc.scalar.dma_start(pool_out, tail[:, :]).then_inc(out_small, 16)
            for c in range(KA):
                if c == 2:
                    ahead(U_POOL - 1, U_POOL - 1)
                small_ready(act, used, full, U_POOL, 0, c)
                nc.scalar.activation(b_hi[:, tt(c)], acc[c % BANKS][:, 0:T], ACT.Copy,
                                     scale=pscale[:, c:c + 1]).then_inc(bh, 1)
            ahead(U_POOL, U_POOL)
            step(STEPS - 1)
            act.wait_ge(at_qk, NG)
            act.wait_ge(out_small, 16 * 5)
            nc.scalar.dma_start(h[:, :], x).then_inc(h_in, 16)

            with act.Fori(0, KA // 2, 1) as jj:
                for g in range(2):
                    at = U_MIX + g * MIX
                    u, j = jj * (2 * MIX) + at, jj * 2 + g
                    for s in range(4):
                        ahead(u + s, at + s)
                        act.wait_ge(taken, j * 8 + (C_MIX + s + 1))
                        nc.scalar.activation(sg[:, tt(s)], sg[:, tt(s)], ACT.Sigmoid).then_inc(ms, 1)
                    ahead(u + 4, at + 4)
                    ahead(u + 5, at + 5)
            act.wait_ge(used, 2 * U_OUT)
            nc.scalar.dma_start(p_raw[:, :], p_in).then_inc(p_loaded, 16)

            def finish(n, c, g, high, parity):
                square(n, parity)
                nc.scalar.activation(high[:, tt(c)], duo(tv, parity), ACT.Copy, scale=gain(g, c)).then_inc(fh, 1)
                nc.scalar.activation(h[:, tt(c)], duo(tv, parity), ACT.Copy).then_inc(hc, 1)

            def square(n, parity):
                act.wait_ge(fa, n + 1)
                nc.scalar.activation(duo(sq, parity), duo(tv, parity), ACT.Square).then_inc(fs, 1)

            def out_chunks(first, end):
                with fours(act, first, end) as i:
                    for s in range(4):
                        ahead(i + (U_OUT + s), U_OUT + s)
                        act.wait_ge(taken, i + (C_OUT + s + 1))
                        finish(i + s, i + s, G_MLP, xa_hi, s % 2)

            out_chunks(0, KD - 4)
            act.wait_ge(p_loaded, 16)
            for k in range(KP):
                nc.scalar.activation(p_hi[:, tt(k)], p_raw[:, tt(k)], ACT.Copy).then_inc(eh, 1)
            out_chunks(KD - 4, KD)

            def embed(u, n):
                for o in range(KD // 2):
                    c = n * (KD // 2) + o
                    small_ready(act, used, full, u, 1 + n, o)
                    if o >= 2:
                        act.wait_ge(taken, (C_P0, C_P1)[n] + o - 1)
                    if o % 2:
                        nc.scalar.activation(e[:, tt(c)], acc[o % BANKS][:, 0:T], ACT.Copy)
                    nc.scalar.activation(duo(sq, o % 2), acc[o % BANKS][:, 0:T], ACT.Square).then_inc(e_s, 1)
                    if o % 4 == 3:
                        ahead(u, u, [o // 4])

            act.wait_ge(fa, 2 + KD)
            embed(U_P0, 0)
            root(1, sumsq, r)
            act.wait_ge(taken, C_MLP)

            def up(u0, c0, n, at):
                with fours(act, 0, KF) as i:
                    for s in range(4):
                        ahead(i + u0 + s, at + s)
                        act.wait_ge(taken, i + c0 + (s + 1))
                        act.wait_ge(ul, i + n + (s + 1))
                        nc.scalar.activation(duo(sq, s % 2), duo(tv, s % 2), ACT.Square)
                        nc.scalar.activation(xb_hi[:, bass.ds((i + s) * T, T)], duo(tv, s % 2),
                                             ACT.Square).then_inc(uh, 1)

            with act.Fori(0, FB - 1, 1) as b:
                up(b * (2 * KF) + U_MLP, b * (2 * KF) + C_MLP, b * KF, U_MLP)
                with fours(act, 0, KF) as i:
                    for s in range(4):
                        ahead(b * (2 * KF) + i + (U_MLP + KF + s), U_MLP + KF + s)
            act.wait_ge(ul, 2 + (FB - 1) * KF)
            embed(U_P1, 1)
            act.wait_ge(taken, C_LAST)
            up(U_LAST, C_LAST, (FB - 1) * KF, U_LAST)
            act.wait_ge(ul, 2 + FB * KF)
            with fours(act, 0, KD) as i:
                for s in range(4):
                    ahead(i + (U_LAST + KF + s), U_LAST + KF + s)
                    act.wait_ge(taken, i + (C_LAST + KF + s + 1))
                    finish(i + (KD + s), i + s, G_PLE, xa_hi, s % 2)
            ahead(U_GATE, U_GATE)
            root(2, sumsq, r)
            root(3, esum, re)

            def gate(n, parity):
                act.wait_ge(taken, n + (C_GATE + 1))
                nc.scalar.activation(duo(tv, parity), duo(tv, parity), ACT.Sigmoid).then_inc(gs, 1)
                if isinstance(n, int) and n == KD - 1:
                    nc.scalar.activation(sg[:, 0:1], ones[:, 0:1], ACT.Sqrt)
                act.wait_ge(gv, 3 * n + 3)
                square(n + 2 * KD, parity)
                nc.scalar.activation(h[:, tt(n)], duo(tv, parity), ACT.Copy, scale=gain(G_FIN, n)).then_inc(hc, 1)

            for c in range(4):
                if c:
                    ahead(U_GATE + c, U_GATE + c)
                gate(c, c % 2)
            with fours(act, 4, KD - 4) as i:
                for s in range(4):
                    ahead(i + (U_GATE + s), U_GATE + s)
                    gate(i + s, s % 2)
            for c in range(KD - 4, KD):
                if c < KD - AHEAD:
                    ahead(U_GATE + c, U_GATE + c)
                gate(c, c % 2)
            root(4, sumsq, r)
            for i, (a, z) in enumerate(Y_PARTS):
                act.wait_ge(yv, i + 1)
                nc.scalar.dma_start(y[:, a * T:z * T], h[:, a * T:z * T]).then_inc(y_out, 16)
            act.wait_ge(y_out, 16 * len(Y_PARTS))

        @block.vector
        def _(dve):
            def split(u, at, halves=range(2)):
                for half in halves:
                    dve.wait_ge(hi_done, 2 * u + (half + 1))
                    dst = (2 * (at % 2) + half) * HALF
                    src = (at % RAW) * UNIT + half * HALF
                    nc.vector.tensor_tensor(w_lo[:, dst:dst + HALF], raw[:, src:src + HALF],
                                            w_hi[:, dst:dst + HALF], ALU.subtract).then_inc(lo_done, 1)

            def ahead(u, at, halves=range(2)):
                split(u + AHEAD, at + AHEAD, halves)

            def factor(n, var, out):
                dve.wait_ge(n_mm, n + 1)
                nc.vector.tensor_scalar(var[:, :], m_ps[:, 0:T], 1.0 / D, EPS, ALU.mult, ALU.add).then_inc(n_var, 1)
                dve.wait_ge(n_std, n + 1)
                nc.vector.reciprocal(out[:, :], out[:, :]).then_inc(n_r, 1)
                dve.wait_ge(n_r, 4 * n + 1)
                nc.vector.tensor_tensor(var[:, :], var[:, :], out[:, :], ALU.mult).then_inc(n_r, 1)
                dve.wait_ge(n_r, 4 * n + 2)
                nc.vector.scalar_tensor_tensor(out=var[:, :], in0=var[:, :], scalar=-0.5, in1=out[:, :],
                                               op0=ALU.mult, op1=ALU.mult).then_inc(n_r, 1)
                dve.wait_ge(n_r, 4 * n + 3)
                nc.vector.scalar_tensor_tensor(out=out[:, :], in0=var[:, :], scalar=1.5, in1=out[:, :],
                                               op0=ALU.add, op1=ALU.mult).then_inc(n_r, 1)
                dve.wait_ge(n_r, 4 * n + 4)

            def clear_sum(n):
                nc.vector.memset(sumsq[:, :], 0.0).then_inc(zero, 1)
                dve.wait_ge(zero, n + 1)

            nc.vector.memset(ones[:, :], 1.0).then_inc(hc, 2)
            dve.wait_ge(hc, 2)
            nc.vector.memset(sumsq[:, :], 0.0).then_inc(fill, 1)
            nc.vector.memset(esum[:, :], 0.0).then_inc(ml, 2)
            dve.wait_ge(ml, 2)
            nc.vector.memset(pline[:, PL_P - HIST:PL_P], 0.0).then_inc(fa, 2)
            nc.vector.memset(pline[:, PL + PL_P - HIST:PL + PL_P], 0.0).then_inc(ul, 2)
            dve.wait_ge(fill, 1)
            dve.wait_ge(fa, 2)
            dve.wait_ge(ul, 2)
            for c in range(KD):
                dve.wait_ge(xh, c + 1)
                nc.vector.scalar_tensor_tensor(out=xa_lo[:, tt(c)], in0=h[:, tt(c)], scalar=gain(G_MIX, c),
                                               in1=xa_hi[:, tt(c)], op0=ALU.mult, op1=ALU.subtract).then_inc(xl, 1)
                if c in (3, 7):
                    split(0, 0, [c // 4])
            split(1, 1)
            for c in range(KD):
                dve.wait_ge(xs, c + 1)
                if c:
                    dve.wait_ge(xadd, c)
                nc.vector.tensor_tensor(sumsq[:, :], sumsq[:, :], duo(sq, c % 2), ALU.add).then_inc(xadd, 1)
                if c == KD // 2:
                    ahead(0, 0)
            ahead(1, 1)
            factor(0, sumsq, r)
            clear_sum(0)
            for n, line in enumerate((kx, vx)):
                for p in range(NPAIR):
                    u = n * NPAIR + p
                    dve.wait_ge(used, 2 * u + 2)
                    at = p * KX
                    nc.vector.memset(line[:, at + 2 * CHUNK:at + 3 * CHUNK], 0.0)
                    nc.vector.tensor_tensor(line[:, at + CHUNK:at + 2 * CHUNK], acc[u][:, 0:DEC], r[:, 0:DEC], ALU.mult)
                    nc.vector.tensor_tensor(line[:, at + 3 * CHUNK:at + KX], acc[u][:, DEC:T], r[:, DEC:T],
                                            ALU.mult).then_inc(taken, 1)
                    if u >= 2:
                        ahead(u, u)

            def queries(u):
                dve.wait_ge(used, 2 * u + 2)
                nc.vector.tensor_tensor(q[:, tt(u - U_Q)], acc[u % BANKS][:, 0:T], r[:, :], ALU.mult).then_inc(taken, 1)
                ahead(u, u)

            for u in range(U_Q, U_STEP):
                queries(u)

            small = [0]

            def link(ins):
                small[0] += 1
                ins.then_inc(at_c, 1)
                dve.wait_ge(at_c, small[0])

            def step(i):
                if 0 <= i - 3 < NG:
                    g = i - 3
                    b, p = GROUPS[g]
                    dve.wait_ge(at_h, g + 1)
                    rows, cols = slice(p * QPP, (p + 1) * QPP), slice(b * CHUNK, (b + 1) * CHUNK)
                    nc.vector.tensor_tensor(a_lo[:, :].rearrange("p (c t) -> p c t", c=KA)[:, rows, cols],
                                            o_ps[:, 0:QPP * CHUNK].rearrange("p (c t) -> p c t", c=QPP),
                                            a_hi[:, :].rearrange("p (c t) -> p c t", c=KA)[:, rows, cols],
                                            ALU.subtract).then_inc(at_l, 1)
                if 0 <= i - 1 < NG:
                    g = i - 1
                    mine = slice(g * QPP, (g + 1) * QPP)
                    dve.wait_ge(at_e, g + 1)
                    link(nc.vector.tensor_tensor(rs[:, mine], rs[:, mine], es[:, mine], ALU.add))
                    link(nc.vector.reciprocal(rec[:, mine], rs[:, mine]))
                    pg = prob[:, (g % 3) * QPP * KEYS:(g % 3 + 1) * QPP * KEYS].rearrange("p (c k) -> p c k", c=QPP)
                    nc.vector.tensor_tensor(pg, pg, rec[:, mine].unsqueeze(2).broadcast_to([P, QPP, KEYS]),
                                            ALU.mult).then_inc(at_p, 1)
                if i < NG:
                    b, p = GROUPS[i]
                    mine = slice(i * QPP, (i + 1) * QPP)
                    pg = prob[:, (i % 3) * QPP * KEYS:(i % 3 + 1) * QPP * KEYS]
                    pg3 = pg.rearrange("p (c k) -> p c k", c=QPP)
                    dve.wait_ge(at_qk, i + 1)
                    if i >= 3:
                        dve.wait_ge(at_t, i - 2)
                    nc.vector.scalar_tensor_tensor(
                        out=pg, in0=s_ps[:, :], scalar=HD ** -0.5,
                        in1=bias[:, p * QPP * KEYS:(p + 1) * QPP * KEYS], op0=ALU.mult, op1=ALU.add).then_inc(at_s, 1)
                    dve.wait_ge(at_s, i + 1)
                    if b == 1:
                        link(nc.vector.memset(pg3[:, :, 0:CHUNK], MASK))
                    link(nc.vector.tensor_reduce(mx[:, mine], pg3, AX.X, ALU.max))
                    link(nc.vector.tensor_tensor(mx[:, mine], mx[:, mine], sink[:, p * QPP:(p + 1) * QPP], ALU.max))
                    link(nc.vector.tensor_scalar(neg[:, mine], mx[:, mine], -1.0, None, ALU.mult))
                    nc.vector.tensor_tensor(es[:, mine], sink[:, p * QPP:(p + 1) * QPP], neg[:, mine],
                                            ALU.add).then_inc(at_m, 1)

            def pool_mean(c):
                w = POOL_W[c // 2]
                line = pline[:, (c % 2) * PL:(c % 2 + 1) * PL]
                k = (DOUBLINGS[c] - 1) % 2
                sums = pacc[:, k * PL:(k + 1) * PL]
                out = duo(tv, c % 2)
                dve.wait_ge(dbl, DOUBLED[c])
                for a, z in ((PL_S, PL_S + DEC), (PL_P + HIST, PL)):
                    nc.vector.scalar_tensor_tensor(
                        out=out[:, a - HIST:z - HIST] if a == PL_S else out[:, DEC + HIST:T], in0=sums[:, a:z],
                        scalar=1.0 / w, in1=line[:, a:z], op0=ALU.mult, op1=ALU.subtract)
                g = c // 2
                nc.vector.tensor_tensor(pfix[:, :], sums[:, PL_P:PL_P + HIST], icnt[:, g * HIST:(g + 1) * HIST],
                                        ALU.mult).then_inc(p_d, 1)
                dve.wait_ge(p_d, 2 * c + 1)
                nc.vector.tensor_tensor(out[:, DEC:DEC + HIST], pfix[:, :], line[:, PL_P:PL_P + HIST],
                                        ALU.subtract).then_inc(p_d, 1)

            def pool_low(c):
                dve.wait_ge(ph, c + 1)
                nc.vector.tensor_tensor(d_lo[:, tt(c)], duo(tv, c % 2), d_hi[:, tt(c)], ALU.subtract).then_inc(pl, 1)

            dve.wait_ge(const_in, CONSTS)
            for u in range(U_STEP, U_U):
                queries(u)
                step(u - U_STEP)
            for u in range(U_U, U_POOL):
                c = u - U_U
                dve.wait_ge(used, 2 * u + 2)
                if c >= 2:
                    dve.wait_ge(line_s, c - 1)
                line = pline[:, (c % 2) * PL:(c % 2 + 1) * PL]
                ps = acc[u % BANKS]
                nc.vector.tensor_tensor(line[:, PL_S:PL_S + DEC], ps[:, 0:DEC], r[:, 0:DEC], ALU.mult)
                nc.vector.tensor_tensor(line[:, PL_P:PL], ps[:, DEC:T], r[:, DEC:T], ALU.mult).then_inc(taken, 1)
                if c:
                    pool_mean(c - 1)
                    pool_low(c - 1)
                if c < KA - 1:
                    ahead(u, u)
                    step(u - U_STEP)
            pool_mean(KA - 1)
            pool_low(KA - 1)
            step(STEPS - 2)
            for c in range(KA):
                if c == 2:
                    ahead(U_POOL - 1, U_POOL - 1)
                dve.wait_ge(bh, c + 1)
                nc.vector.scalar_tensor_tensor(out=b_lo[:, tt(c)], in0=acc[c % BANKS][:, 0:T], scalar=pscale[:, c:c + 1],
                                               in1=b_hi[:, tt(c)], op0=ALU.mult, op1=ALU.subtract).then_inc(taken, 1)
            ahead(U_POOL, U_POOL)
            step(STEPS - 1)

            with dve.Fori(0, KA // 2, 1) as jj:
                for g in range(2):
                    at = U_MIX + g * MIX
                    u, j = jj * (2 * MIX) + at, jj * 2 + g
                    c0 = j * 8 + C_MIX
                    dve.wait_ge(ml, j * 2 + 2)
                    for s in range(4):
                        dve.wait_ge(used, 2 * u + (2 * s + 2))
                        nc.vector.tensor_tensor(sg[:, tt(s)], acc[s][:, 0:T], r[:, :], ALU.mult).then_inc(taken, 1)
                        ahead(u + s, at + s)
                    for s in range(2):
                        dve.wait_ge(used, 2 * u + (2 * 4 + s + 1))
                        dve.wait_ge(ms, j * 4 + (s + 1))
                        nc.vector.tensor_tensor(sg[:, tt(s)], acc[s][:, 0:T], sg[:, tt(s)], ALU.mult).then_inc(taken, 1)
                    ahead(u + 4, at + 4)
                    for s in range(2):
                        dve.wait_ge(used, 2 * u + (2 * 5 + s + 1))
                        dve.wait_ge(ms, j * 4 + (2 + s + 1))
                        nc.vector.tensor_tensor(sg[:, tt(2 + s)], acc[2 + s][:, 0:T], sg[:, tt(2 + s)],
                                                ALU.mult).then_inc(taken, 1)
                        dve.wait_ge(taken, c0 + (6 + s + 1))
                        m = bass.ds((j * 2 + s) * T, T)
                        nc.vector.tensor_tensor(xb_hi[:, m], sg[:, tt(s)], sg[:, tt(2 + s)], ALU.add)
                        nc.vector.tensor_tensor(sg[:, tt(s)], sg[:, tt(s)], sg[:, tt(2 + s)], ALU.add).then_inc(mv, 1)
                        dve.wait_ge(mv, j * 2 + (s + 1))
                        nc.vector.tensor_tensor(xb_lo[:, m], sg[:, tt(s)], xb_hi[:, m], ALU.subtract).then_inc(ml, 1)
                    ahead(u + 5, at + 5)

            def residual(c, bank, out):
                nc.vector.tensor_tensor(out, h[:, tt(c)], acc[bank][:, 0:T], ALU.add).then_inc(taken, 1)

            def finish(n, c, g, high, low, parity):
                dve.wait_ge(fh, n + 1)
                nc.vector.scalar_tensor_tensor(out=low[:, tt(c)], in0=duo(tv, parity), scalar=gain(g, c),
                                               in1=high[:, tt(c)], op0=ALU.mult, op1=ALU.subtract).then_inc(fl, 1)
                add_square(n, parity)

            def add_square(n, parity):
                dve.wait_ge(fs, n + 1)
                dve.wait_ge(fa, n + 2)
                nc.vector.tensor_tensor(sumsq[:, :], sumsq[:, :], duo(sq, parity), ALU.add).then_inc(fa, 1)

            dve.wait_ge(h_in, 16)
            def out_chunks(first, end):
                with fours(dve, first, end) as i:
                    for s in range(4):
                        c = i + s
                        dve.wait_ge(used, 2 * i + (2 * (U_OUT + s) + 2))
                        dve.wait_ge(hc, c + 1)
                        residual(c, s, duo(tv, s % 2))
                        ahead(i + (U_OUT + s), U_OUT + s)
                        finish(c, c, G_MLP, xa_hi, xa_lo, s % 2)

            out_chunks(0, KD - 4)
            for k in range(KP):
                dve.wait_ge(eh, k + 1)
                nc.vector.tensor_tensor(p_lo[:, tt(k)], p_raw[:, tt(k)], p_hi[:, tt(k)], ALU.subtract).then_inc(el, 1)
            out_chunks(KD - 4, KD)

            def embed(u, n):
                for o in range(KD // 2):
                    c = n * (KD // 2) + o
                    dve.wait_ge(e_s, c + 1)
                    if o % 2 == 0:
                        nc.vector.tensor_copy(e[:, tt(c)], acc[o % BANKS][:, 0:T])
                    dve.wait_ge(taken, (C_P0, C_P1)[n] + o)
                    nc.vector.tensor_tensor(esum[:, :], esum[:, :], duo(sq, o % 2), ALU.add).then_inc(taken, 1)
                    if o % 4 == 3:
                        ahead(u, u, [o // 4])

            embed(U_P0, 0)
            factor(1, sumsq, r)
            clear_sum(1)

            def up(u0, c0, n, at):
                with fours(dve, 0, KF) as i:
                    for s in range(4):
                        dve.wait_ge(used, 2 * i + 2 * u0 + (2 * s + 2))
                        nc.vector.scalar_tensor_tensor(out=duo(tv, s % 2), in0=acc[s][:, 0:T], scalar=0.0,
                                                       in1=r[:, :], op0=ALU.max, op1=ALU.mult).then_inc(taken, 1)
                        ahead(i + u0 + s, at + s)
                        dve.wait_ge(uh, i + n + (s + 1))
                        m = bass.ds((i + s) * T, T)
                        nc.vector.tensor_tensor(xb_lo[:, m], duo(sq, s % 2), xb_hi[:, m], ALU.subtract).then_inc(ul, 1)

            with dve.Fori(0, FB - 1, 1) as b:
                up(b * (2 * KF) + U_MLP, b * (2 * KF) + C_MLP, b * KF, U_MLP)
                with fours(dve, 0, KF) as i:
                    for s in range(4):
                        u = b * (2 * KF) + i + (U_MLP + KF + s)
                        dve.wait_ge(used, 2 * u + 2)
                        residual(i + s, s, h[:, tt(i + s)])
                        ahead(u, U_MLP + KF + s)
            embed(U_P1, 1)
            up(U_LAST, C_LAST, (FB - 1) * KF, U_LAST)
            with fours(dve, 0, KD) as i:
                for s in range(4):
                    dve.wait_ge(used, 2 * i + (2 * (U_LAST + KF + s) + 2))
                    dve.wait_ge(hc, i + (KD + s + 1))
                    residual(i + s, s, duo(tv, s % 2))
                    ahead(i + (U_LAST + KF + s), U_LAST + KF + s)
                    finish(i + (KD + s), i + s, G_PLE, xa_hi, xa_lo, s % 2)
            ahead(U_GATE, U_GATE)
            factor(2, sumsq, r)
            clear_sum(2)
            factor(3, esum, re)

            def ple_chunk(n, bank, between=None):
                parity = bank % 2
                dve.wait_ge(hc, n + (2 * KD + 1))
                dve.wait_ge(used, 2 * n + (2 * U_GATE + 2))
                nc.vector.tensor_tensor(duo(tv, parity), acc[bank][:, 0:T], r[:, :], ALU.mult).then_inc(taken, 1)
                if between:
                    between()
                nc.vector.scalar_tensor_tensor(out=ple[:, :], in0=e[:, tt(n)], scalar=gain(G_POST, n), in1=re[:, :],
                                               op0=ALU.mult, op1=ALU.mult).then_inc(gv, 1)
                dve.wait_ge(gv, 3 * n + 1)
                dve.wait_ge(gs, n + 1)
                nc.vector.tensor_tensor(ple[:, :], ple[:, :], duo(tv, parity), ALU.mult).then_inc(gv, 1)
                dve.wait_ge(gv, 3 * n + 2)
                nc.vector.tensor_tensor(duo(tv, parity), h[:, tt(n)], ple[:, :], ALU.add).then_inc(gv, 1)
                add_square(n + 2 * KD, parity)

            for c in range(4):
                ple_chunk(c, c, (lambda: ahead(U_GATE + c, U_GATE + c)) if c else None)
            with fours(dve, 4, KD - 4) as i:
                for s in range(4):
                    ple_chunk(i + s, s, lambda: ahead(i + (U_GATE + s), U_GATE + s))
            for c in range(KD - 4, KD):
                ple_chunk(c, c % BANKS, (lambda: ahead(U_GATE + c, U_GATE + c)) if c < KD - AHEAD else None)
            factor(4, sumsq, r)
            dve.wait_ge(hc, 2 + 3 * KD)
            for a, z in Y_PARTS:
                part = h[:, a * T:z * T].rearrange("p (c t) -> p c t", c=z - a)
                nc.vector.tensor_tensor(part, part, r[:, :].unsqueeze(1).broadcast_to([P, z - a, T]),
                                        ALU.mult).then_inc(yv, 1)


def _tiles(w, np):
    i, o = w.shape
    return w.reshape(i // P, P, o // P, P).transpose(2, 1, 0, 3)


def _units(w, np):
    t = _tiles(w, np)
    per = TILES // t.shape[2]
    n = t.shape[0] // per
    return t.reshape(n, per, P, t.shape[2], P).transpose(0, 2, 1, 3, 4).reshape(n, P, UNIT)


def kernel(**inputs):
    import numpy as np
    import concourse.bacc as bacc
    from concourse.bass_utils import run_bass_kernel_spmd

    a = {k: np.asarray(v) for k, v in inputs.items()}

    heads = [8 * p + 4 * s + c for p in range(NPAIR) for c in range(QPP) for s in range(2)]
    qcols = np.concatenate([np.arange(hd * HD, (hd + 1) * HD) for hd in heads])
    width = KA * P // len(POOL_W)
    pcols = np.arange(KA * P).reshape(len(POOL_W), width)[::-1].ravel()
    w_in = a["w_in"][0]
    o = np.cumsum([0, NH * HD, NKV * HD, NKV * HD, KA * P, D, D])
    part = [w_in[:, o[n]:o[n + 1]] for n in range(6)]
    ga, gb = _units(part[4], np), _units(part[5], np)
    ba, bb = _units(a["w_branch_a"][0][qcols], np), _units(a["w_branch_b"][0][pcols], np)
    stream = [_units(part[1], np), _units(part[2], np), _units(part[0][:, qcols], np), _units(part[3][:, pcols], np)]
    pg = a["pool_group_w"][0][::-1].reshape(len(POOL_W), 2, P, 2, P).transpose(2, 0, 3, 1, 4)
    stream.append(pg.reshape(1, P, UNIT))
    for j in range(KA):
        stream += [ga[2 * j:2 * j + 2], gb[2 * j:2 * j + 2], ba[j:j + 1], bb[j:j + 1]]
    stream.append(_units(a["w_out"][0], np))
    proj = _units(a["w_ple_proj"][0], np)
    stream.append(proj[0:1])
    up = _units(a["w_up"][0], np)
    down = a["w_down"][0].reshape(FB, FF // FB, D)
    for b in range(FB):
        if b == FB - 1:
            stream.append(proj[1:2])
        stream += [up[b * KF:(b + 1) * KF], _units(down[b], np)]
    stream.append(_units(a["w_ple_gate"][0], np))
    weights = np.concatenate(stream).reshape(UNITS * P, UNIT)

    def feature_major(s, p):
        t = np.concatenate([s, p]).T
        return np.ascontiguousarray(t.reshape(-1, P, T).transpose(1, 0, 2)).reshape(P, -1)

    def cols(v):
        return v.reshape(-1, P).T

    slope = np.power(np.float32(2.0), np.float32(-8.0) * np.arange(1, NH + 1, dtype=np.float32) / NH)
    dist = np.abs(CHUNK + np.arange(CHUNK)[:, None] - np.arange(KEYS)[None, :]).astype(np.float32)
    alibi = np.stack([-slope[hd] * dist for hd in heads]).astype(np.float32)
    alibi = alibi.reshape(KA, 2 * CHUNK, KEYS).transpose(1, 0, 2).reshape(P, KA * KEYS)
    count = np.minimum(np.array(POOL_W)[:, None], np.arange(1, HIST + 1)[None, :])
    inv_count = np.broadcast_to((1.0 / count).astype(np.float32).reshape(1, -1), (P, len(POOL_W) * HIST))
    sinks = a["attn_sinks"][0][heads].reshape(KA, 2)
    sinks = np.repeat(sinks[:, :, None], CHUNK, axis=2).reshape(KA, P).T

    def cached(c):
        return c[0, 0].reshape(KEYS, NKV * HD)[CHUNK:].T

    arrays = {
        "x": feature_major(a["x_sample"][0], a["x_prompt"][0]),
        "cache_k": cached(a["cache_k"]), "cache_v": cached(a["cache_v"]),
        "hist": a["state_pool"][0, 0].T[pcols].reshape(KA, P, HIST).transpose(1, 0, 2).reshape(P, -1),
        "p_in": feature_major(a["p_sample"][0, 0], a["p_prompt"][0, 0]),
        "weights": weights,
        "gains": np.concatenate([cols(a["g_mix"][0]), cols(a["g_mlp"][0]), cols(a["g_ple"][0]),
                                 cols(a["g_ple_post"][0]), cols(a["g_final"])], axis=1),
        "post_scale": cols(a["pool_scale"][0][pcols]), "sinks": sinks, "alibi": alibi, "inv_count": inv_count,
        "ident_in": np.eye(P, dtype=np.float32),
    }
    outs = {"y": (P, KD * T), "kv_prompt": (2, NPAIR * P, KEYS), "kv_sample": (2, NPAIR * P, KEYS),
            "pool_out": (P, KA * 2 * HIST)}

    nc = bacc.Bacc("TRN2", target_bir_lowering=False, num_devices=1, dynamic_dma_scratch_size=1024)
    args, sent = {}, {}
    for name, v in arrays.items():
        v = np.ascontiguousarray(v)
        sent[f"in_{name}"] = v
        args[name] = nc.dram_tensor(f"in_{name}", v.shape, mybir.dt.from_np(v.dtype), kind="ExternalInput").ap()
    for name, shape in outs.items():
        args[name] = nc.dram_tensor(f"out_{name}", shape, F32, kind="ExternalOutput").ap()
    encoder_step(nc, **args)
    got = run_bass_kernel_spmd(nc, [sent], core_ids=[0]).results[0]

    yt = got["out_y"].reshape(P, KD, T).transpose(2, 1, 0).reshape(T, D)

    def rows(v):
        return v.T.reshape(1, 1, KEYS, NKV, HD)

    pool = got["out_pool_out"].reshape(P, KA, 2, HIST).transpose(2, 3, 1, 0).reshape(2, 1, 1, HIST, KA * P)[..., np.argsort(pcols)]
    kp, ks = got["out_kv_prompt"], got["out_kv_sample"]
    res = (yt[DEC:].reshape(1, SEQ, D), yt[:DEC].reshape(1, DEC, D), rows(kp[0]), rows(kp[1]), pool[1],
           rows(ks[0]), rows(ks[1]), pool[0])
    return tuple(np.ascontiguousarray(v) for v in res)
```
